# Optimizing a Trainium2 kernel written in Bass

```python
import math
import jax, jax.numpy as jnp
from jax import lax
import numpy as np

D_MODEL = 1024
BATCH = 1
SEQ = 512
DEPTH = 1

N_HEADS = 8
N_KV_HEADS = 2
HEAD_DIM = 64
Q_PER_KV = N_HEADS // N_KV_HEADS
ROT_DIM = HEAD_DIM // 4
ROPE_THETA = 500000.0
CMP_LEN = 32
CMP_STRIDE = 16
CMP_HIDDEN = 256
SLC_LEN = 64
SLC_TOPK = 16
WINDOW = 512
Q_BLOCK = 128
ATTN_WIDTH = N_HEADS * HEAD_DIM
KV_WIDTH = N_KV_HEADS * HEAD_DIM
SSM_WIDTH = 512
SSM_GROUP = 16
SSM_GROUPS = SSM_WIDTH // SSM_GROUP
SSM_STATE = 64
SSM_CHUNK = 128
D_FF = 2816
CONV_WIDTH = 3
EPS = 1e-6
NEG_INF = -1e30
FORCE_SCORE = 1e4

IN_SIZES = (ATTN_WIDTH, KV_WIDTH, KV_WIDTH, KV_WIDTH, KV_WIDTH, KV_WIDTH, KV_WIDTH,
            3 * N_HEADS, SSM_WIDTH, D_MODEL, D_MODEL)
IN_OFFSETS = tuple(int(v) for v in np.cumsum(IN_SIZES)[:-1])
D_IN = int(sum(IN_SIZES))

kernel_name = "hybrid_nsa_s5_convffn_block"

def rmsnorm(x, g):
    xf = x.astype(jnp.float32)
    r = xf * lax.rsqrt(jnp.mean(xf * xf, axis=-1, keepdims=True) + EPS)
    return (r * g.astype(jnp.float32)).astype(x.dtype)

def partial_rope(x, pos):
    half = ROT_DIM // 2
    inv_freq = ROPE_THETA ** (-jnp.arange(0, ROT_DIM, 2, dtype=jnp.float32) / ROT_DIM)
    ang = pos.astype(jnp.float32)[..., None] * inv_freq
    cos = jnp.cos(ang)[:, :, None, :].astype(x.dtype)
    sin = jnp.sin(ang)[:, :, None, :].astype(x.dtype)
    x1, x2, rest = x[..., :half], x[..., half:ROT_DIM], x[..., ROT_DIM:]
    return jnp.concatenate([x1 * cos - x2 * sin, x2 * cos + x1 * sin, rest], axis=-1)

def masked_softmax(s, mask, axis):
    s = jnp.where(mask, s.astype(jnp.float32), NEG_INF)
    m = jnp.max(s, axis=axis, keepdims=True)
    e = jnp.where(mask, jnp.exp(s - m), 0.0)
    return e / jnp.maximum(jnp.sum(e, axis=axis, keepdims=True), 1e-30)

def cmp_block_ends(seq):
    n_cmp = (seq - CMP_LEN) // CMP_STRIDE + 1
    return jnp.arange(n_cmp, dtype=jnp.int32) * CMP_STRIDE + CMP_LEN - 1, n_cmp

def compress(kraw, pe, w1, w2, n_cmp):
    idx = jnp.arange(n_cmp)[:, None] * CMP_STRIDE + jnp.arange(CMP_LEN)[None, :]
    blocks = kraw[:, idx] + pe[None, None, :, None, :]
    b, n, l, kh, d = blocks.shape
    flat = blocks.transpose(0, 1, 3, 2, 4).reshape(b, n, kh, l * d)
    return jax.nn.gelu(flat @ w1) @ w2

def nsa_attention(q, k_cmp, v_cmp, k_slc, v_slc, k_win, v_win, gates, cmp_end):
    bsz, seq = q.shape[0], q.shape[1]
    nb = seq // Q_BLOCK
    n_slc = seq // SLC_LEN
    topk = min(SLC_TOPK, n_slc)
    c_start = cmp_end - (CMP_LEN - 1)
    s_start = jnp.arange(n_slc, dtype=jnp.int32) * SLC_LEN
    ov = jnp.minimum(c_start[:, None] + CMP_LEN, s_start[None, :] + SLC_LEN) - jnp.maximum(c_start[:, None], s_start[None, :])
    overlap = jnp.clip(ov, 0, None).astype(jnp.float32) / CMP_LEN
    ks_blocks = k_slc.reshape(bsz, n_slc, SLC_LEN, N_KV_HEADS, HEAD_DIM).transpose(0, 3, 1, 2, 4)
    vs_blocks = v_slc.reshape(bsz, n_slc, SLC_LEN, N_KV_HEADS, HEAD_DIM).transpose(0, 3, 1, 2, 4)
    pad = ((0, 0), (WINDOW, 0), (0, 0), (0, 0))
    kw_p, vw_p = jnp.pad(k_win, pad), jnp.pad(v_win, pad)
    q_blocks = q.reshape(bsz, nb, Q_BLOCK, N_KV_HEADS, Q_PER_KV, HEAD_DIM).transpose(1, 0, 2, 3, 4, 5)
    g_blocks = gates.reshape(bsz, nb, Q_BLOCK, N_KV_HEADS, Q_PER_KV, 3).transpose(1, 0, 2, 3, 4, 5)
    b_idx = jnp.arange(bsz)[:, None, None, None]
    h_idx = jnp.arange(N_KV_HEADS)[None, :, None, None]
    j_idx = jnp.arange(n_slc, dtype=jnp.int32)

    def block(args):
        c, qb, gb = args
        t = c * Q_BLOCK + jnp.arange(Q_BLOCK, dtype=jnp.int32)
        s_c = jnp.einsum('bqkgd,bnkd->bkgqn', qb, k_cmp)
        mask_c = (cmp_end[None, :] <= t[:, None])[None, None, None]
        p_c = masked_softmax(s_c, mask_c, axis=-1)
        o_c = jnp.einsum('bkgqn,bnkd->bqkgd', p_c.astype(v_cmp.dtype), v_cmp)
        imp = jnp.einsum('bkgqn,nj->bqkj', p_c, overlap)
        forced = (j_idx[None, :] == 0) | (j_idx[None, :] == (t // SLC_LEN)[:, None])
        valid = (j_idx[None, :] * SLC_LEN) <= t[:, None]
        score = jnp.where(forced[None, :, None, :], FORCE_SCORE, imp)
        score = jnp.where(valid[None, :, None, :], score, NEG_INF)
        top_val, top_idx = lax.top_k(score, topk)
        sel_ok = (top_val > 0.5 * NEG_INF).transpose(0, 2, 1, 3)
        top_idx_t = top_idx.transpose(0, 2, 1, 3)
        ks = ks_blocks[b_idx, h_idx, top_idx_t]
        vs = vs_blocks[b_idx, h_idx, top_idx_t]
        s_s = jnp.einsum('bkgqd,bkqnsd->bkgqns', qb.transpose(0, 2, 3, 1, 4), ks)
        tok = top_idx_t[..., None] * SLC_LEN + jnp.arange(SLC_LEN, dtype=jnp.int32)
        mask_s = (sel_ok[..., None] & (tok <= t[None, None, :, None, None]))[:, :, None]
        p_s = masked_softmax(s_s, mask_s, axis=(-2, -1))
        o_s = jnp.einsum('bkgqns,bkqnsd->bqkgd', p_s.astype(vs.dtype), vs)
        kw = lax.dynamic_slice_in_dim(kw_p, c * Q_BLOCK, Q_BLOCK + WINDOW, axis=1)
        vw = lax.dynamic_slice_in_dim(vw_p, c * Q_BLOCK, Q_BLOCK + WINDOW, axis=1)
        s_w = jnp.einsum('bqkgd,bjkd->bkgqj', qb, kw)
        kpos = c * Q_BLOCK - WINDOW + jnp.arange(Q_BLOCK + WINDOW, dtype=jnp.int32)
        diff = t[:, None] - kpos[None, :]
        mask_w = ((kpos[None, :] >= 0) & (diff >= 0) & (diff < WINDOW))[None, None, None]
        p_w = masked_softmax(s_w, mask_w, axis=-1)
        o_w = jnp.einsum('bkgqj,bjkd->bqkgd', p_w.astype(vw.dtype), vw)
        o = gb[..., 0:1] * o_c + gb[..., 1:2] * o_s + gb[..., 2:3] * o_w
        return o.reshape(bsz, Q_BLOCK, ATTN_WIDTH).astype(q.dtype)

    out = lax.map(block, (jnp.arange(nb, dtype=jnp.int32), q_blocks, g_blocks))
    return out.transpose(1, 0, 2, 3).reshape(bsz, seq, ATTN_WIDTH)

def s5_layer(u, a_re, a_im, b_re, b_im, c_re, c_im, d_skip, log_dt, w_glu):
    bsz, seq = u.shape[0], u.shape[1]
    nc = seq // SSM_CHUNK
    f32 = jnp.float32
    A = lax.complex(a_re.astype(f32), a_im.astype(f32))
    dt = jnp.exp(log_dt.astype(f32))[:, None]
    A_bar = jnp.exp(A * dt)
    B_bar = ((A_bar - 1.0) / A)[..., None] * lax.complex(b_re.astype(f32), b_im.astype(f32))
    Cm = lax.complex(c_re.astype(f32), c_im.astype(f32))
    uf = u.astype(f32)
    uc = uf.reshape(bsz, nc, SSM_CHUNK, SSM_GROUPS, SSM_GROUP).transpose(1, 2, 0, 3, 4)
    a_chunk = jnp.broadcast_to(A_bar, (SSM_CHUNK, bsz, SSM_GROUPS, SSM_STATE))

    def op(e1, e2):
        a1, b1 = e1
        a2, b2 = e2
        return a1 * a2, a2 * b1 + b2

    def step(carry, u_c):
        bu = jnp.einsum('cbgh,gph->cbgp', u_c.astype(jnp.complex64), B_bar)
        a_cum, x_loc = lax.associative_scan(op, (a_chunk, bu), axis=0)
        xs = x_loc + a_cum * carry[None]
        y = jnp.real(jnp.einsum('ghp,cbgp->cbgh', Cm, xs))
        return xs[-1], y

    carry0 = jnp.zeros((bsz, SSM_GROUPS, SSM_STATE), jnp.complex64)
    _, ys = lax.scan(step, carry0, uc)
    y = ys.transpose(2, 0, 1, 3, 4).reshape(bsz, seq, SSM_WIDTH) + d_skip.astype(f32) * uf
    y = jax.nn.gelu(y)
    y = y * jax.nn.sigmoid(y @ w_glu.astype(f32))
    return y.astype(u.dtype)

def causal_dwconv(x, w, b):
    seq = x.shape[1]
    xp = jnp.pad(x, ((0, 0), (CONV_WIDTH - 1, 0), (0, 0)))
    out = b
    for k in range(CONV_WIDTH):
        out = out + w[k] * xp[:, k:k + seq]
    return out

def setup_inputs(seed: int = 0) -> dict:
    key = jax.random.key(seed)
    ks = jax.random.split(key, 32)
    nrm = lambda k, shape, s: jax.random.normal(k, shape, jnp.float32) * s
    L = DEPTH
    n_idx = jnp.arange(SSM_STATE, dtype=jnp.float32)
    return {
        "x": nrm(ks[0], (BATCH, SEQ, D_MODEL), 1.0),
        "positions": jnp.broadcast_to(jnp.arange(SEQ, dtype=jnp.int32), (BATCH, SEQ)),
        "norm_mix": 1.0 + nrm(ks[1], (L, D_MODEL), 0.02),
        "w_in": nrm(ks[2], (L, D_MODEL, D_IN), D_MODEL ** -0.5),
        "cmp_k_pe": nrm(ks[3], (L, CMP_LEN, HEAD_DIM), 0.02),
        "cmp_k_w1": nrm(ks[4], (L, CMP_LEN * HEAD_DIM, CMP_HIDDEN), (CMP_LEN * HEAD_DIM) ** -0.5),
        "cmp_k_w2": nrm(ks[5], (L, CMP_HIDDEN, HEAD_DIM), CMP_HIDDEN ** -0.5),
        "cmp_v_pe": nrm(ks[6], (L, CMP_LEN, HEAD_DIM), 0.02),
        "cmp_v_w1": nrm(ks[7], (L, CMP_LEN * HEAD_DIM, CMP_HIDDEN), (CMP_LEN * HEAD_DIM) ** -0.5),
        "cmp_v_w2": nrm(ks[8], (L, CMP_HIDDEN, HEAD_DIM), CMP_HIDDEN ** -0.5),
        "ssm_a_re": -0.5 + nrm(ks[9], (L, SSM_GROUPS, SSM_STATE), 0.01),
        "ssm_a_im": math.pi * n_idx + nrm(ks[10], (L, SSM_GROUPS, SSM_STATE), 0.01),
        "ssm_b_re": nrm(ks[11], (L, SSM_GROUPS, SSM_STATE, SSM_GROUP), (2.0 * SSM_GROUP) ** -0.5),
        "ssm_b_im": nrm(ks[12], (L, SSM_GROUPS, SSM_STATE, SSM_GROUP), (2.0 * SSM_GROUP) ** -0.5),
        "ssm_c_re": nrm(ks[13], (L, SSM_GROUPS, SSM_GROUP, SSM_STATE), (2.0 * SSM_STATE) ** -0.5),
        "ssm_c_im": nrm(ks[14], (L, SSM_GROUPS, SSM_GROUP, SSM_STATE), (2.0 * SSM_STATE) ** -0.5),
        "ssm_d": nrm(ks[15], (L, SSM_WIDTH), 0.5),
        "ssm_log_dt": jax.random.uniform(ks[16], (L, SSM_GROUPS), jnp.float32, math.log(1e-3), math.log(1e-1)),
        "ssm_w_glu": nrm(ks[17], (L, SSM_WIDTH, SSM_WIDTH), SSM_WIDTH ** -0.5),
        "w_proj_a": nrm(ks[18], (L, ATTN_WIDTH, D_MODEL), ATTN_WIDTH ** -0.5),
        "w_proj_b": nrm(ks[19], (L, SSM_WIDTH, D_MODEL), SSM_WIDTH ** -0.5),
        "w_out": nrm(ks[20], (L, D_MODEL, D_MODEL), D_MODEL ** -0.5),
        "norm_ffn": 1.0 + nrm(ks[21], (L, D_MODEL), 0.02),
        "w_up": nrm(ks[22], (L, D_MODEL, 2 * D_FF), D_MODEL ** -0.5),
        "conv_w": nrm(ks[23], (L, CONV_WIDTH, 2 * D_FF), CONV_WIDTH ** -0.5),
        "conv_b": nrm(ks[24], (L, 2 * D_FF), 0.01),
        "w_down": nrm(ks[25], (L, D_FF, D_MODEL), D_FF ** -0.5),
        "norm_final": 1.0 + nrm(ks[26], (D_MODEL,), 0.02),
    }

def reference(x, positions, norm_mix, w_in, cmp_k_pe, cmp_k_w1, cmp_k_w2, cmp_v_pe, cmp_v_w1, cmp_v_w2,
              ssm_a_re, ssm_a_im, ssm_b_re, ssm_b_im, ssm_c_re, ssm_c_im, ssm_d, ssm_log_dt, ssm_w_glu,
              w_proj_a, w_proj_b, w_out, norm_ffn, w_up, conv_w, conv_b, w_down, norm_final):
    bsz, seq = x.shape[0], x.shape[1]
    cmp_end, n_cmp = cmp_block_ends(seq)
    cmp_pos = positions[:, cmp_end]
    kv_shape = (bsz, seq, N_KV_HEADS, HEAD_DIM)
    for l in range(DEPTH):
        h = rmsnorm(x, norm_mix[l])
        proj = h @ w_in[l]
        q, kc, vc, ksl, vsl, kwn, vwn, ng, u, ga, gb = jnp.split(proj, IN_OFFSETS, axis=-1)
        q = partial_rope(q.reshape(bsz, seq, N_HEADS, HEAD_DIM), positions) * (HEAD_DIM ** -0.5)
        k_cmp = partial_rope(compress(kc.reshape(kv_shape), cmp_k_pe[l], cmp_k_w1[l], cmp_k_w2[l], n_cmp), cmp_pos)
        v_cmp = compress(vc.reshape(kv_shape), cmp_v_pe[l], cmp_v_w1[l], cmp_v_w2[l], n_cmp)
        k_slc = partial_rope(ksl.reshape(kv_shape), positions)
        k_win = partial_rope(kwn.reshape(kv_shape), positions)
        nsa_gates = jax.nn.sigmoid(ng.reshape(bsz, seq, N_HEADS, 3))
        y_a = nsa_attention(q, k_cmp, v_cmp, k_slc, vsl.reshape(kv_shape), k_win, vwn.reshape(kv_shape),
                            nsa_gates, cmp_end)
        y_b = s5_layer(u, ssm_a_re[l], ssm_a_im[l], ssm_b_re[l], ssm_b_im[l], ssm_c_re[l], ssm_c_im[l],
                       ssm_d[l], ssm_log_dt[l], ssm_w_glu[l])
        merged = jax.nn.sigmoid(ga) * (y_a @ w_proj_a[l]) + jax.nn.sigmoid(gb) * (y_b @ w_proj_b[l])
        x = x + merged @ w_out[l]
        h2 = rmsnorm(x, norm_ffn[l])
        up = causal_dwconv(h2 @ w_up[l], conv_w[l], conv_b[l])
        gate, val = jnp.split(up, 2, axis=-1)
        x = x + (jax.nn.silu(gate) * val) @ w_down[l]
    return rmsnorm(x, norm_final)


_drawn_inputs = setup_inputs


def setup_inputs(seed=0):
    import zlib

    import numpy as np

    out = dict(_drawn_inputs(seed))
    spreads = {}
    factors = {'norm_mix': 8.0,
     'cmp_k_pe': 8.0,
     'cmp_v_pe': 42.773,
     'ssm_a_re': 64.0,
     'ssm_a_im': 38.44,
     'ssm_b_re': 53.656,
     'ssm_b_im': 54.584,
     'ssm_c_re': 53.024,
     'ssm_c_im': 53.752,
     'ssm_log_dt': 38.92,
     'ssm_w_glu': 3.55,
     'norm_ffn': 3.647,
     'conv_b': 7.707,
     'norm_final': 7.819}
    for name, (base, spread) in spreads.items():
        noise = np.random.default_rng([zlib.crc32(name.encode()), seed]).standard_normal(out[name].shape)
        drawn = base * np.exp(spread * noise) if base else spread * noise
        out[name] = __import__('jax').numpy.asarray(drawn.astype(out[name].dtype))
    for name, factor in factors.items():
        out[name] = (out[name] * factor).astype(out[name].dtype)
    return out
```

```python
from contextlib import ExitStack
import math

import numpy as np

import concourse.bass as bass
from concourse import mybir
from concourse.alu_op_type import AluOpType as ALU

ACT = mybir.ActivationFunctionType
F32 = mybir.dt.float32
F32R = mybir.dt.float32r
BF16 = mybir.dt.bfloat16
I32 = mybir.dt.int32
AX = mybir.AxisListType.X

P = 128
T = 512
D = 1024
KT = D // P
NQT = T // P
HD = 64
NKV = 2
REP = 4
NCMP = 31
NCP = 32
DFF = 2816
UPC = DFF // P
NSSM = 512
G = 32
GH = 16
NST = 64
TC = 8
NC = T // TC
NP = G // 2
HP = NP // 2
EPS = 1e-6
NEG = -1e30
RING = 4
TWO_PI = 2 * math.pi
C1 = 6.28125
C2 = float(np.float32(np.floor((TWO_PI - C1) * 2 ** 21) / 2 ** 21))
C3 = float(np.float32(TWO_PI - C1 - C2))
MAGIC = 1.5 * 2 ** 23
LN2H = float(np.float32(355.0 / 512.0))
LN2L = float(np.float32(math.log(2) - 355.0 / 512.0))

U_V = 0
U_KC, U_VC = 3, 4
U_U = 5
U_W1K = (9, 11, 13, 15)
U_W1V = (17, 19, 20, 22)
U_KSL, U_KWN = 10, 12
U_Q = (14, 16, 18, 21)
U_G = 23
U_GLU = 39
U_M = 41
U_O = 49
U_UP = 57
U_DN = 101
NU = 125
VN = 256 + 24

CST = {}
PRE = {}
LATE = {}


def _columns(table, names):
    at = 0
    for name, n in names:
        table[name] = (at, at + n)
        at += n
    return at


N_CST = _columns(CST, [("ident", P), ("perm", P), ("causal", P), ("cadd", NQT * 64), ("c01", NQT * 64),
                       ("freq", 1), ("eye16", GH)])
N_PRE = _columns(PRE, [("ldt", NP), ("are", NP), ("aim", NP), ("bre", NP * GH), ("bim", NP * GH),
                       ("cre", NP * GH), ("cim", NP * GH), ("w2k", 2 * HD), ("w2v", 2 * HD),
                       ("pek", 16), ("pev", 16), ("d", G)])
N_LATE = _columns(LATE, [("gmix", KT), ("gffn", KT), ("gfin", KT), ("cw", 2 * UPC * 3), ("cb", 2 * UPC)])


class Count:

    def __init__(self, eng, sem, start=0):
        self.eng, self.sem, self.n, self.reg, self.per, self.at = eng, sem, start, None, 0, 0

    def inc(self, ins):
        ins.then_inc(self.sem, 1)
        self.n += 1
        return ins

    def wait(self, back=0):
        value = self.n - back
        self.eng.wait_ge(self.sem, value if self.reg is None else self.reg * self.per + value)

    def step(self, ins):
        self.inc(ins)
        self.wait()

    def enter(self, reg, per):
        self.reg, self.per, self.at = reg, per, self.n

    def leave(self, times):
        assert self.n - self.at == self.per, (self.n - self.at, self.per)
        self.n = self.at + self.per * times
        self.reg = None


def build(nc, wst, xT, cst_d, pre_d, late_d, pos_d, outT):
    with ExitStack() as ctx:
        def at(name, shape, dt, offset):
            return nc.alloc_sbuf_tensor_at(name, shape, dt, offset=offset)

        def sem(name):
            return ctx.enter_context(nc.semaphore(name))

        K = 1024
        B0 = 16 * K
        x32 = at("x32", [P, KT, T], F32, B0)
        hh = at("hh", [P, KT, T], F32R, B0 + 16 * K)
        hl = at("hl", [P, KT, T], F32R, B0 + 32 * K)
        wh = at("wh", [P, RING, KT, P], F32R, B0 + 48 * K)
        wl = at("wl", [P, RING, KT, P], F32R, B0 + 64 * K)
        wf = at("wf", [P, RING, KT, P], F32, B0 + 80 * K)
        late = at("late", [P, N_LATE], F32, B0 + 96 * K)
        cst = at("cst", [P, N_CST], F32, B0 + 97 * K)
        ones = at("ones", [P, P], F32, B0 + 101 * K)
        R0 = B0 + 102 * K
        q32 = at("q32", [P, REP, T], F32, R0)
        ksh = at("ksh", [P, 2, NKV, T], F32R, R0 + 8 * K)
        ksl = at("ksl", [P, 2, NKV, T], F32R, R0 + 16 * K)
        vst = at("vst", [P, NQT, 2 * NKV, P], F32R, R0 + 24 * K)
        kch = at("kch", [P, NKV, NCP], F32R, R0 + 32 * K)
        kcl = at("kcl", [P, NKV, NCP], F32R, R0 + 32 * K + 256)
        vcs = at("vcs", [2 * NCP, NKV, P], F32R, R0 + 32 * K + 512)
        gt = at("gt", [P, NQT, 24], F32, R0 + 33 * K + 512)
        identb = at("identb", [P, P], BF16, R0 + 34 * K)
        maskb = at("maskb", [P, P], BF16, R0 + 34 * K + 256)
        R1 = R0 + 34 * K + 512
        pre = at("pre", [P, N_PRE], F32, R1)
        cosT = at("cosT", [P, T], F32, R1 + 6 * K)
        sinT = at("sinT", [P, T], F32, R1 + 8 * K)
        xr = at("xr", [P, 2, T], F32, R1 + 10 * K)
        rt = at("rt", [P, 2, T], F32, R1 + 14 * K)
        skip = at("skip", [P, G, GH], F32, R1 + 22 * K)
        x2 = at("x2", [P, NKV, T], F32, R1 + 18 * K)
        fl32 = at("fl32", [P, 16, NKV, NCMP], F32, R1 + 26 * K)
        flh = at("flh", [P, 17, NKV, NCMP], F32R, R1 + 30 * K)
        fll = at("fll", [P, 17, NKV, NCMP], F32R, R1 + 30 * K + 4224)
        htok = [at("htok0", [NKV * NCMP, 256], F32, R0 + 6 * K), at("htok1", [NKV * NCMP, 256], F32, R1 + 30 * K)]
        kcs = at("kcs", [P, NCMP], F32, R0 + 33 * K + 896)
        g32 = at("g32", [P, 2, NKV, NCMP], F32, R1 + 5568)
        sm = at("sm", [P, 32, NP], F32, R1 + 38 * K + 512)
        pw = at("pw", [P, 2, TC + 1, NP], F32, R1 + 40 * K + 512)
        bbar = at("bbar", [P, 2, NP, GH], F32, R1 + 24 * K)
        bb = at("bb", [P, 2, 2, NP, GH], F32, R1 + 42 * K - 256)
        ltab = at("ltab", [P, 2, HP, TC + 1, GH], F32, R1 + 46 * K - 256)
        ttab = at("ttab", [P, 2, HP, P], F32, R1 + 55 * K - 256)
        vre = at("vre", [P, 2, HP, NC], F32, R1 + 63 * K - 256)
        uin = at("uin", [P, 2 * HP, NC], F32, R1 + 67 * K + 256)
        rtab = at("rtab", [P, 2, HP, NC], F32, R1 + 18 * K)
        w2t = at("w2t", [P, 2, HP, P], F32, B0)
        ksb = at("ksb", [GH, 2 * HP, P], F32, B0)
        mtab = at("mtab", [P, 2 * HP, P], F32, B0 + 8 * K)
        atmp = at("atmp", [P, HP * (TC + 1) * GH], F32, R1 + 63 * K - 256)
        xs = at("xs", [P, 2, 2, HP, NC], F32, R1 + 55 * K - 256)
        ysb = at("ysb", [P, 2 * HP, NC], F32, R1 + 26 * K)
        uperm = at("uperm", [P, 2, TC, NC], F32, R1 + 10 * K)
        posi = at("posi", [P, T], I32, R1 + 22 * K)

        bank = [ctx.enter_context(nc.psum_tensor(f"bank{i}", [P, 512], F32)) for i in range(8)]
        u_scr = nc.dram_tensor("u_scr", (NSSM, TC, NC), F32, kind="Internal").ap()
        y_scr = nc.dram_tensor("y_scr", (NSSM, TC, NC), F32, kind="Internal").ap()

        def psum(i, *dims):
            v = bank[i][:]
            if not dims:
                return v
            n = int(np.prod(dims))
            names = "abcd"[:len(dims)]
            return v[:, 0:n].rearrange(f"p ({' '.join(names)}) -> p {' '.join(names)}",
                                       **dict(zip(names, dims)))

        def c(name, rows=slice(None)):
            return cst[rows, CST[name][0]:CST[name][1]]

        def pr(name, rows=slice(None)):
            return pre[rows, PRE[name][0]:PRE[name][1]]

        def lt(name):
            return late[:, LATE[name][0]:LATE[name][1]]

        x_in = [sem(f"x_in{i}") for i in range(4)]
        pre_in, cst_in, late_in, pos_in = sem("pre_in"), sem("cst_in"), sem("late_in"), sem("pos_in")
        x_back = sem("x_back")
        w_in = [sem(f"w_in{i}") for i in range(RING)]
        w_hi, w_lo, w_used = sem("w_hi"), sem("w_lo"), sem("w_used")
        sq_ok, ss_ok = sem("sq_ok"), sem("ss_ok")
        var_ok, sd_ok = sem("var_ok"), sem("sd_ok")
        ones_ok, zero_ok = sem("ones_ok"), sem("zero_ok")
        h_ok, hh_ok, hl_ok = sem("h_ok"), sem("hh_ok"), sem("hl_ok")
        dve, act = sem("dve"), sem("act")
        ang_ok, trig_ok = sem("ang_ok"), sem("trig_ok")
        bf_ok = sem("bf_ok")
        v_hi, v_lo = sem("v_hi"), sem("v_lo")
        out_ok = sem("out_ok")
        fl_ok, flh_ok, fll_ok = sem("fl_ok"), sem("flh_ok"), sem("fll_ok")
        hid_ok, hidt_ok = sem("hid_ok"), sem("hidt_ok")
        gelu_ok = sem("gelu_ok")
        vc_ok = sem("vc_ok")
        cmp_ok, cmpe_ok = sem("cmp_ok"), sem("cmpe_ok")
        perm_ok, roped = sem("perm_ok"), sem("roped")
        kh_ok = sem("kh_ok")
        u_put = [sem(f"u_put{i}") for i in range(4)]
        u_get = sem("u_get")
        sk_ok = sem("sk_ok")
        w2_ok, tr_ok, t_ok = sem("w2_ok"), sem("tr_ok"), sem("t_ok")
        l_ok, kk_ok, kse_ok = sem("l_ok"), sem("kk_ok"), sem("kse_ok")
        m_in = sem("m_in")
        vm_ok, ve_ok, xs_ok = sem("vm_ok"), sem("ve_ok"), sem("xs_ok")
        ym_ok, ye_ok, y_put, y_in = sem("ym_ok"), sem("ye_ok"), sem("y_put"), sem("y_in")

        FEAT = [U_KC, U_VC] + [U_U + i for i in range(4)]
        FEAT += [U_KSL, U_KWN] + list(U_Q)
        place = {u: n for n, u in enumerate(FEAT)}
        rope_place = {u: n for n, u in enumerate([U_KSL, U_KWN] + list(U_Q))}
        ROPE_CMP = 4

        P_AT = (0, 128, 384, 768)
        S_AT = ((2, 384), (3, 0), (2, 0), (1, 0))
        PT_AT = ((4, 0), (5, 0), (6, 0), (5, 384))
        PS_AT = (0, 512, 1024, 896)
        BANKS = ((3,), (2, 0), (1,))
        yah = at("yah", [P, REP, T], F32R, R1)
        yal = at("yal", [P, REP, T], F32R, R1 + 8 * K)
        qs = at("qs", [P, NKV, T], F32R, R1 + 16 * K)
        prob = at("prob", [P, 1280], F32, R1 + 20 * K)
        pc = at("pc", [P, NQT, NKV, NCP], F32, R1 + 31 * K)
        small = at("small", [P, 40], F32, R1 + 32 * K)
        olo = at("olo", [P, T], F32, R1 + 33 * K)
        y32 = at("y32", [P, T], F32, R1 + 35 * K)
        graw = at("graw", [P, 2 * KT, T], F32, R1 + 39 * K)
        pth = at("pth", [P, 1280], F32R, B0)
        ptl = at("ptl", [P, 1280], F32R, B0 + 5 * K)
        pcth = at("pcth", [2 * NCP, T], F32R, B0 + 10 * K)
        pctl = at("pctl", [2 * NCP, T], F32R, B0 + 12 * K)
        nmx, sums, scale = small[:, 0:4], small[:, 4:8], small[:, 8:12]
        cmx, csum = small[:, 16:24], small[:, 24:32]
        signal = at("signal", [P, 8], F32, B0 + 101 * K + 576)
        q_hi, q_lo = sem("q_hi"), sem("q_lo")
        s_ok = sem("s_ok")
        mx_ok, cm_ok = sem("mx_ok"), sem("cm_ok")
        e_ok, ec_ok = sem("e_ok"), sem("ec_ok")
        p_ok, pc_ok = sem("p_ok"), sem("pc_ok")
        pt_ok = sem("pt_ok")
        pth_ok, ptl_ok = sem("pth_ok"), sem("ptl_ok")
        pch_ok, pcl_ok = sem("pch_ok"), sem("pcl_ok")
        o_ok, ol_ok, o_free = sem("o_ok"), sem("ol_ok"), sem("o_free")
        g_ok = sem("g_ok")
        yl_ok = sem("yl_ok")

        yraw = at("yraw", [P, 4, TC, NC], F32, R0)
        yg = at("yg", [P, 4, T], F32, R0 + 8 * K)
        ygh = at("ygh", [P, 4, T], F32R, R0 + 16 * K)
        ygl = at("ygl", [P, 4, T], F32R, R0 + 24 * K)
        ybh = at("ybh", [P, 4, T], F32R, R0)
        ybl = at("ybl", [P, 4, T], F32R, R1 + 16 * K)
        yb = at("yb", [P, 2, T], F32, R1 + 25 * K)
        ygelu, ygh_ok, ygl_ok = sem("ygelu"), sem("ygh_ok"), sem("ygl_ok")
        glu_ok, glus_ok = sem("glu_ok"), sem("glus_ok")
        yb_ok, ybh_ok, ybl_ok = sem("yb_ok"), sem("ybh_ok"), sem("ybl_ok")

        sgl = at("sgl", [P, 2, T], F32, R1 + 29 * K)
        mt = at("mt", [P, 2, 2, T], F32, R0 + 16 * K)
        mgh = at("mgh", [P, KT, T], F32R, R1 + 39 * K)
        mgl = at("mgl", [P, KT, T], F32R, R1 + 55 * K)
        sg_ok, mg_ok = sem("sg_ok"), sem("mg_ok")
        ml_ok = sem("ml_ok")

        T0 = R0 + 88 * K
        gth = at("gth", [P, UPC, T], F32R, R0)
        gtl = at("gtl", [P, UPC, T], F32R, R0 + 44 * K)
        raw = at("raw", [P, 4, 2 + T], F32, T0)
        cv = at("cv", [P, 2, T], F32, T0 + 8 * K + 256)
        sl = at("sl", [P, T], F32, T0 + 12 * K + 256)
        sq2 = at("sq2", [P, T], F32, R0 + 8 * K)
        acc = at("acc", [P, T], F32, R0 + 12 * K)
        acc3 = at("acc3", [P, T], F32, T0 + 4 * K)
        nt = at("nt", [P, 3, T], F32, R0 + 24 * K)
        nt3 = at("nt3", [P, 3, T], F32, T0 + 6 * K)
        rs = at("rs", [P, T], F32, B0 + 98 * K)
        x1_ok, acc_ok, ss2_ok = sem("x1_ok"), sem("acc_ok"), sem("ss2_ok")
        x2l_ok = sem("x2l_ok")
        var2_ok, sd2_ok = sem("var2_ok"), sem("sd2_ok")
        raw_ok, cv_ok, sl_ok, gg_ok = sem("raw_ok"), sem("cv_ok"), sem("sl_ok"), sem("gg_ok")
        gh_ok, gl_ok = sem("gh_ok"), sem("gl_ok")
        x2_ok, fin_ok, out_put = sem("x2_ok"), sem("fin_ok"), sem("out_put")

        def store_output(sp):
            for o in range(KT):
                sp.wait_ge(fin_ok, o + 1)
                sp.dma_start(outT[:, o, :], x32[:, o]).then_inc(out_put, 16)
            sp.wait_ge(out_put, 16 * KT)

        def tensor_attention_to_end(pe, ready, three):
            M = nc.tensor
            pe.wait_ge(roped, 7)
            pe.wait_ge(ye_ok, 4)
            pe.wait_ge(vc_ok, 2)
            pe.wait_ge(gelu_ok, 4)
            pe.wait_ge(xs_ok, 2)
            pe.wait_ge(bf_ok, 1)
            pe.wait_ge(out_ok, 12)
            with pe.Fori(0, REP, 1) as r:
                def gates_part(j, part):
                    s = (U_G + j) % RING
                    if part == 0:
                        pe.wait_ge(w_lo, r * 4 + (U_G + j + 1))
                        pe.wait_ge(g_ok, r * 4 + (j + 1))
                    for k in range(4 * part, 4 * part + 4):
                        ins = three(psum(0), wh[:, s, k], wl[:, s, k], hh[:, k], hl[:, k], k == 0, k == KT - 1)
                    if part:
                        ins.then_inc(w_used, 1)

                def scores(i):
                    kv, b = i // 2, i % 2
                    if i == 0:
                        pe.wait_ge(q_hi, r * 2 + 2)
                        pe.wait_ge(q_lo, r * 2 + 2)
                        for t in range(NQT):
                            for kv_ in range(NKV):
                                out = psum(3)[:, 256 + 64 * t + 32 * kv_:256 + 64 * t + 32 * kv_ + 32]
                                M.matmul(out, qs[:, kv_, P * t:P * t + P], kch[:, kv_], start=True, stop=False)
                                M.matmul(out, qs[:, kv_, P * t:P * t + P], kcl[:, kv_], start=False, stop=True)
                    for tiles in BANKS:
                        for t in tiles:
                            bk, at_ = S_AT[t]
                            n = P * (t + 1)
                            out = psum(bk)[:, at_:at_ + n]
                            M.matmul(out, qs[:, kv, P * t:P * t + P], ksh[:, b, kv, 0:n], start=True, stop=False)
                            M.matmul(out, qs[:, kv, P * t:P * t + P], ksl[:, b, kv, 0:n], start=False, stop=False)
                            ins = M.matmul(out[:, n - P:n], identb[:], maskb[:], start=False, stop=True)
                        ins.then_inc(s_ok, 1)

                def transposes(i):
                    if i == 1:
                        pe.wait_ge(pc_ok, r + 1)
                    pe.wait_ge(p_ok, r * 4 + (i + 1))
                    for kt in (0, 1, 3, 2):
                        if i == 1 and kt == 2:
                            for t in range(NQT):
                                M.matmul(psum(6)[64 * (t // 2):64 * (t // 2) + 64,
                                                 256 + P * (t % 2):256 + P * (t % 2) + P],
                                         pc[:, t].rearrange("p a b -> p (a b)"), c("ident"), start=True, stop=True)
                        bk, at_ = PT_AT[kt]
                        for t in range(kt, NQT):
                            col = at_ + P * (t - kt)
                            ins = M.transpose(psum(bk)[:, col:col + P], prob[:, P_AT[t] + P * kt:P_AT[t] + P * kt + P],
                                              c("ident"))
                        if kt != 1:
                            ins.then_inc(pt_ok, 1)

                def values_product(i):
                    kv, b = i // 2, i % 2
                    if b == 0:
                        pe.wait_ge(o_free, r * 2 + (kv + 1))
                    pe.wait_ge(pth_ok, r * 12 + 3 * (i + 1))
                    pe.wait_ge(ptl_ok, r * 12 + 3 * (i + 1))
                    for kt in range(NQT):
                        n = T - P * kt
                        for x_ in (pth, ptl):
                            ins = M.matmul(psum(7)[:, P * kt:T], vst[:, kt, 2 * b + kv], x_[:, PS_AT[kt]:PS_AT[kt] + n],
                                           start=(b == 0 and kt == 0 and x_ is pth), stop=False)
                    if b:
                        pe.wait_ge(pch_ok, r * 2 + 2)
                        pe.wait_ge(pcl_ok, r * 2 + 2)
                        M.matmul(psum(7), vcs[:, kv], pcth[:], start=False, stop=False)
                        M.matmul(psum(7), vcs[:, kv], pctl[:], start=False, stop=True).then_inc(o_ok, 1)

                gates_part(0, 0)
                scores(0)
                gates_part(0, 1)
                transposes(0)
                scores(1)
                gates_part(1, 0)
                values_product(0)
                gates_part(1, 1)
                transposes(1)
                scores(2)
                gates_part(2, 0)
                values_product(1)
                gates_part(2, 1)
                transposes(2)
                scores(3)
                gates_part(3, 0)
                values_product(2)
                transposes(3)
                gates_part(3, 1)
                values_product(3)

            for n in range(4):
                u, s = U_GLU + n // 2, (U_GLU + n // 2) % RING
                if n % 2 == 0:
                    ready(u)
                if n == 0:
                    pe.wait_ge(g_ok, 17)
                for k in range(4):
                    if n == 0:
                        pe.wait_ge(ygl_ok, k + 1)
                    ins = three(psum(n), wh[:, s, 4 * (n % 2) + k], wl[:, s, 4 * (n % 2) + k], ygh[:, k], ygl[:, k],
                                k == 0, k == 3)
                ins.then_inc(glu_ok if n % 2 == 0 else w_used, 1)

            pe.wait_ge(o_free, 9)
            with pe.Fori(0, 2, 1) as b:
                for j in range(4):
                    s = (U_M + j) % RING
                    pe.wait_ge(w_lo, b * 4 + (U_M + j + 1))
                    if j == 0:
                        pe.wait_ge(yl_ok, 4)
                    pe.wait_ge(mg_ok, b * 4 + (j + 1))
                    for k in range(4):
                        three(psum(4 + 2 * (j % 2)), wh[:, s, k], wl[:, s, k], yah[:, k], yal[:, k], k == 0, k == 3)
                    if j == 0:
                        pe.wait_ge(ybl_ok, 4)
                    for k in range(4):
                        ins = three(psum(5 + 2 * (j % 2)), wh[:, s, 4 + k], wl[:, s, 4 + k], ybh[:, k], ybl[:, k],
                                    k == 0, k == 3)
                    ins.then_inc(w_used, 1)

            with pe.Fori(0, 2, 1) as b:
                for j in range(4):
                    s = (U_O + j) % RING
                    pe.wait_ge(w_lo, b * 4 + (U_O + j + 1))
                    pe.wait_ge(x1_ok, b * 4 + (j + 1))
                    for k in range(KT):
                        if j == 0:
                            pe.wait_ge(ml_ok, k + 1)
                        ins = three(psum(j % 2), wh[:, s, k], wl[:, s, k], mgh[:, k], mgl[:, k], k == 0, k == KT - 1)
                    ins.then_inc(w_used, 1)
            pe.wait_ge(mg_ok, 10)
            pe.wait_ge(acc_ok, 1)
            M.matmul(psum(7), ones[:], acc[:], start=True, stop=True).then_inc(ss2_ok, 1)

            pe.wait_ge(glus_ok, 4)
            with pe.Fori(0, UPC // 2, 1) as b:
                for j in range(4):
                    s = (U_UP + j) % RING
                    pe.wait_ge(w_lo, b * 4 + (U_UP + j + 1))
                    pe.wait_ge(raw_ok, b * 4 + (j + 1))
                    for k in range(KT):
                        if j == 0:
                            pe.wait_ge(x2l_ok, k + 1)
                        ins = three(psum(2 + j % 2), wh[:, s, k], wl[:, s, k], hh[:, k], hl[:, k], k == 0, k == KT - 1)
                    ins.then_inc(w_used, 1)

            with pe.Fori(0, 2, 1) as b:
                for o in range(4):
                    pe.wait_ge(x2_ok, b * 4 + (o + 1))
                    for m in range(3):
                        v_ = 3 * o + m
                        s = (U_DN + v_) % RING
                        pe.wait_ge(w_lo, b * 12 + (U_DN + v_ + 1))
                        for k in range(8 * m, min(8 * m + 8, UPC)):
                            if o == 0:
                                pe.wait_ge(gl_ok, k + 1)
                            ins = three(psum(o % 2), wh[:, s, k % 8], wl[:, s, k % 8], gth[:, k], gtl[:, k],
                                        k == 0, k == UPC - 1)
                        ins.then_inc(w_used, 1)
            pe.wait_ge(acc_ok, 2)
            M.matmul(psum(7), ones[:], acc3[:], start=True, stop=True).then_inc(ss2_ok, 1)

        def scalar_attention_to_end(a, prep):
            A = nc.scalar
            a.wait_ge(ye_ok, 4)
            a.wait_ge(vc_ok, 2)
            a.wait_ge(xs_ok, 2)

            def prep_next(base, j, reg, per):
                u = base + j + RING
                a.wait_ge(w_in[u % RING], reg * (16 * per // RING) + 16 * (u // RING + 1))
                a.wait_ge(w_used, reg * per + (u - RING + 1))
                A.activation(wh[:, u % RING], wf[:, u % RING], ACT.Copy).then_inc(w_hi, 1)

            with a.Fori(0, REP, 1) as r:
                def exps(i):
                    for n, tiles in enumerate(BANKS):
                        a.wait_ge(mx_ok, r * 12 + (3 * i + n + 1))
                        for t in tiles:
                            bk, at_ = S_AT[t]
                            w_ = P * (t + 1)
                            A.activation(prob[:, P_AT[t]:P_AT[t] + w_], psum(bk)[:, at_:at_ + w_], ACT.Exp,
                                         bias=nmx[:, t:t + 1], scale=1.0, accum_out=sums[:, t:t + 1]).then_inc(e_ok, 1)

                def his(i):
                    for n in range(3):
                        a.wait_ge(pt_ok, r * 12 + (3 * i + n + 1))
                        if i == 1 and n == 2:
                            for half in range(2):
                                A.activation(pcth[:, 256 * half:256 * half + 256],
                                             psum(6)[64 * half:64 * half + 64, 256:512], ACT.Copy).then_inc(pch_ok, 1)
                        w_ = 256 if n == 2 else 512
                        A.activation(pth[:, 512 * n:512 * n + w_], psum(4 + n)[:, 0:w_], ACT.Copy).then_inc(pth_ok, 1)

                def gate_raw(j):
                    prep_next(U_G, j, r, 4)
                    A.activation(graw[:, bass.ds(r * 4 + j, 1), :].rearrange("p a b -> p (a b)"), psum(0),
                                 ACT.Copy).then_inc(g_ok, 1)

                def out_lo(kv):
                    a.wait_ge(o_ok, r * 2 + (kv + 1))
                    a.wait_ge(o_free, r * 2 + (kv + 1))
                    A.activation(olo[0:HD], psum(7)[HD:P], ACT.Copy).then_inc(ol_ok, 1)

                for kv in range(NKV):
                    rows = slice(64 * kv, 64 * kv + 64)
                    A.activation(qs[rows, kv, :], q32[rows, bass.ds(r, 1), :].rearrange("p a b -> p (a b)"), ACT.Copy,
                                 scale=HD ** -0.5).then_inc(q_hi, 1)
                exps(0)
                a.wait_ge(cm_ok, r + 1)
                A.activation(pc[:], pc[:], ACT.Exp).then_inc(ec_ok, 1)
                gate_raw(0)
                his(0)
                exps(1)
                gate_raw(1)
                his(1)
                exps(2)
                out_lo(0)
                gate_raw(2)
                his(2)
                exps(3)
                his(3)
                gate_raw(3)
                out_lo(1)

            a.wait_ge(y_put, 32 * TC)
            a.dma_start(yraw[:], y_scr.rearrange("(i p) j c -> p i j c", p=P)).then_inc(y_in, 16)
            a.dma_start(x32[:], xT).then_inc(x_back, 16)
            a.wait_ge(y_in, 16)
            for i in range(4):
                A.activation(yg[:, i].rearrange("p (c j) -> p j c", j=TC), yraw[:, i],
                             ACT.Gelu_apprx_tanh).then_inc(ygelu, 1)
                a.wait_ge(ygelu, i + 1)
                A.activation(ygh[:, i], yg[:, i], ACT.Copy).then_inc(ygh_ok, 1)

            def gate_sigmoids(blocks):
                for n in blocks:
                    A.activation(graw[:, n:n + KT + 1:KT, :], graw[:, n:n + KT + 1:KT, :],
                                 ACT.Sigmoid).then_inc(sg_ok, 1)

            a.wait_ge(g_ok, 2 * KT + 1)
            gate_sigmoids(range(3))
            a.wait_ge(yl_ok, 4)
            for n in range(4):
                if n % 2:
                    a.wait_ge(w_used, U_GLU + n // 2 + 1)
                else:
                    a.wait_ge(glu_ok, n // 2 + 1)
                if n >= 2:
                    a.wait_ge(yb_ok, n - 1)
                A.activation(sgl[:, n % 2], psum(n), ACT.Sigmoid).then_inc(glus_ok, 1)
                if n % 2:
                    prep(U_GLU + n // 2 + RING)
                a.wait_ge(yb_ok, n + 1)
                A.activation(ybh[:, n], yb[:, n % 2], ACT.Copy).then_inc(ybh_ok, 1)

            gate_sigmoids(range(3, KT))
            with a.Fori(0, (U_UP - U_M) // RING, 1) as b:
                for j in range(RING):
                    prep_next(U_M, j, b, RING)
            a.wait_ge(var2_ok, 1)
            A.activation(nt[:, 1], nt[:, 0], ACT.Sqrt).then_inc(sd2_ok, 1)

            with a.Fori(0, UPC // 2, 1) as b:
                for p_ in range(2):
                    a.wait_ge(cv_ok, b * 2 + (p_ + 1))
                    A.activation(sl[:], cv[:, 0], ACT.Silu).then_inc(sl_ok, 1)
                    prep_next(U_UP, 2 * p_, b, 4)
                    a.wait_ge(gg_ok, b * 2 + (p_ + 1))
                    prep_next(U_UP, 2 * p_ + 1, b, 4)
                    A.activation(gth[:, bass.ds(b * 2 + p_, 1), :].rearrange("p a b -> p (a b)"), sl[:],
                                 ACT.Copy).then_inc(gh_ok, 1)
            with a.Fori(0, (NU - U_DN - RING) // RING, 1) as b:
                for j in range(RING):
                    prep_next(U_DN, j, b, 4)
            a.wait_ge(var2_ok, 2)
            A.activation(nt3[:, 1], nt3[:, 0], ACT.Sqrt).then_inc(sd2_ok, 1)

        def vector_attention_to_end(v, own, tt, ts, stt):
            V = nc.vector
            v.wait_ge(ym_ok, 2)
            v.wait_ge(ye_ok, 4)

            def flat2(ap):
                return ap.rearrange("p a b -> p (a b)")

            V.memset(signal[:, 0:1], 0.0).then_inc(g_ok, 1)
            V.memset(signal[:, 1:2], 0.0).then_inc(o_free, 1)
            for n, both in enumerate((mg_ok, x1_ok, raw_ok, x2_ok)):
                V.memset(signal[:, 2 + n:3 + n], 0.0).then_inc(both, 2)

            with v.Fori(0, REP, 1) as r:
                own.enter(r, 52)

                def maxima(i):
                    for n, tiles in enumerate(BANKS):
                        v.wait_ge(s_ok, r * 12 + (3 * i + n + 1))
                        if i == 0 and n == 2:
                            own.inc(V.tensor_tensor(flat4(pc), psum(3)[:, 256:512], c("cadd"), ALU.add))
                        for t in tiles:
                            bk, at_ = S_AT[t]
                            w_ = P * (t + 1)
                            own.inc(V.tensor_reduce(small[:, 36 + t:37 + t], psum(bk)[:, at_:at_ + w_], AX, ALU.max))
                        own.wait()
                        for m, t in enumerate(tiles):
                            ins = V.tensor_scalar(nmx[:, t:t + 1], small[:, 36 + t:37 + t], -1.0, None, ALU.mult)
                            if m < len(tiles) - 1:
                                own.inc(ins)
                            else:
                                ins.then_inc(mx_ok, 1)

                def scaled(i):
                    kv, b = i // 2, i % 2
                    v.wait_ge(e_ok, r * 16 + 4 * (i + 1))
                    ts(scale, sums, 1e-30, ALU.max)
                    own.step(V.reciprocal(scale, scale))
                    tt(scale, scale, flat2(gt[:, :, bass.ds(r * 2 + (8 * (1 + b) + kv), 1)]), ALU.mult)
                    for t in range(NQT):
                        tile = prob[:, P_AT[t]:P_AT[t] + P * (t + 1)]
                        ins = V.tensor_scalar(tile, tile, scale[:, t:t + 1], None, ALU.mult)
                        if t < NQT - 1:
                            own.inc(ins)
                        else:
                            ins.then_inc(p_ok, 1)

                def los(i):
                    for n in range(3):
                        v.wait_ge(pth_ok, r * 12 + (3 * i + n + 1))
                        cols = slice(512 * n, 512 * n + (256 if n == 2 else 512))
                        V.tensor_tensor(ptl[:, cols], psum(4 + n)[:, 0:cols.stop - cols.start],
                                        pth[:, cols].bitcast(F32), ALU.subtract).then_inc(ptl_ok, 1)
                    if i == 1:
                        v.wait_ge(pch_ok, r * 2 + 2)
                        for half in range(2):
                            cols = slice(256 * half, 256 * half + 256)
                            V.tensor_tensor(pctl[:, cols], psum(6)[64 * half:64 * half + 64, 256:512],
                                            pcth[:, cols].bitcast(F32), ALU.subtract).then_inc(pcl_ok, 1)

                def head_out(kv):
                    v.wait_ge(ol_ok, r * 2 + (kv + 1))
                    V.tensor_tensor(y32[64 * kv:64 * kv + 64], psum(7)[0:HD], olo[0:HD], ALU.add).then_inc(o_free, 1)

                def flat4(x_):
                    return x_[:].rearrange("p a b c -> p (a b c)")

                pc8 = pc[:].rearrange("p a b c -> p (a b) c")
                v.wait_ge(q_hi, r * 2 + 2)
                for kv in range(NKV):
                    rows, other = slice(64 * kv, 64 * kv + 64), slice(64 - 64 * kv, 128 - 64 * kv)
                    V.scalar_tensor_tensor(out=qs[other, kv, :], in0=flat2(q32[rows, bass.ds(r, 1), :]),
                                           scalar=HD ** -0.5, in1=qs[rows, kv, :].bitcast(F32), op0=ALU.mult,
                                           op1=ALU.subtract).then_inc(q_lo, 1)
                maxima(0)
                own.step(V.tensor_reduce(cmx, pc8, AX, ALU.max))
                V.tensor_tensor(pc8, pc8, cmx.unsqueeze(2).to_broadcast([P, 8, NCP]), ALU.subtract).then_inc(cm_ok, 1)
                scaled(0)
                v.wait_ge(ec_ok, r + 1)
                tt(flat4(pc), flat4(pc), c("c01"), ALU.mult)
                own.step(V.tensor_reduce(csum, pc8, AX, ALU.add))
                ts(csum, csum, 1e-30, ALU.max)
                own.step(V.reciprocal(csum, csum))
                c4 = csum.rearrange("p (a b) -> p a b", b=NKV)
                tt(c4, c4, gt[:, :, bass.ds(r * 2, 2)], ALU.mult)
                V.tensor_tensor(pc8, pc8, csum.unsqueeze(2).to_broadcast([P, 8, NCP]), ALU.mult).then_inc(pc_ok, 1)
                los(0)
                maxima(1)
                scaled(1)
                los(1)
                maxima(2)
                scaled(2)
                head_out(0)
                los(2)
                maxima(3)
                scaled(3)
                los(3)
                head_out(1)
                v.wait_ge(o_free, r * 2 + 3)
                own.step(V.tensor_scalar(flat2(yah[:, bass.ds(r, 1), :]), y32[:], 1.0, None, ALU.mult))
                V.tensor_tensor(flat2(yal[:, bass.ds(r, 1), :]), y32[:], flat2(yah[:, bass.ds(r, 1), :]).bitcast(F32),
                                ALU.subtract).then_inc(yl_ok, 1)
            own.leave(REP)

            for i in range(4):
                v.wait_ge(ygh_ok, i + 1)
                V.tensor_tensor(ygl[:, i], yg[:, i], ygh[:, i].bitcast(F32), ALU.subtract).then_inc(ygl_ok, 1)
            for n in range(4):
                v.wait_ge(glus_ok, n + 1)
                V.tensor_tensor(yb[:, n % 2], yg[:, n], sgl[:, n % 2], ALU.mult).then_inc(yb_ok, 1)
                v.wait_ge(ybh_ok, n + 1)
                V.tensor_tensor(ybl[:, n], yb[:, n % 2], ybh[:, n].bitcast(F32), ALU.subtract).then_inc(ybl_ok, 1)

            own.step(V.memset(acc[:], 0.0))
            with v.Fori(0, 2, 1) as b:
                own.enter(b, 12)
                for j in range(4):
                    blk = bass.ds(b * 4 + j, 1)
                    v.wait_ge(w_used, b * 4 + (U_M + j + 1))
                    v.wait_ge(sg_ok, b * 4 + (j + 1))
                    for i in range(2):
                        own.inc(V.tensor_tensor(mt[:, j % 2, i], psum(4 + 2 * (j % 2) + i),
                                                flat2(graw[:, bass.ds(b * 4 + (8 * i + j), 1), :]), ALU.mult))
                    own.wait()
                    V.tensor_tensor(mt[:, j % 2, 0], mt[:, j % 2, 0], mt[:, j % 2, 1], ALU.add).then_inc(mg_ok, 1)
                    v.wait_ge(mg_ok, b * 4 + (j + 3))
                    own.step(V.tensor_scalar(flat2(mgh[:, blk, :]), mt[:, j % 2, 0], 1.0, None, ALU.mult))
                    V.tensor_tensor(flat2(mgl[:, blk, :]), mt[:, j % 2, 0], flat2(mgh[:, blk, :]).bitcast(F32),
                                    ALU.subtract).then_inc(ml_ok, 1)
            own.leave(2)

            v.wait_ge(x_back, 16)
            with v.Fori(0, 2, 1) as b:
                own.enter(b, 12)
                for j in range(4):
                    blk = bass.ds(b * 4 + j, 1)
                    xb = flat2(x32[:, blk, :])
                    v.wait_ge(w_used, b * 4 + (U_O + j + 1))
                    V.tensor_tensor(xb, xb, psum(j % 2), ALU.add).then_inc(x1_ok, 1)
                    v.wait_ge(x1_ok, b * 4 + (j + 3))
                    gain = lt("gffn")[:, blk]
                    own.inc(V.tensor_tensor(sq2[:], xb, xb, ALU.mult))
                    own.step(V.tensor_scalar(flat2(hh[:, blk, :]), xb, gain, None, ALU.mult))
                    V.scalar_tensor_tensor(out=flat2(hl[:, blk, :]), in0=xb, scalar=gain,
                                           in1=flat2(hh[:, blk, :]).bitcast(F32), op0=ALU.mult,
                                           op1=ALU.subtract).then_inc(x2l_ok, 1)
                    own.step(V.tensor_tensor(acc[:], acc[:], sq2[:], ALU.add))
            own.leave(2)
            V.memset(raw[:, :, 0:2], 0.0).then_inc(acc_ok, 1)

            def inverse_rms(n, tmp):
                v.wait_ge(ss2_ok, n)
                V.tensor_scalar(tmp[:, 0], psum(7), 1.0 / D, EPS, ALU.mult, ALU.add).then_inc(var2_ok, 1)
                v.wait_ge(sd2_ok, n)
                own.step(V.reciprocal(rs[:], tmp[:, 1]))
                tt(tmp[:, 2], rs[:], rs[:], ALU.mult)
                tt(tmp[:, 2], tmp[:, 2], tmp[:, 0], ALU.mult)
                ts(tmp[:, 2], tmp[:, 2], -0.5, ALU.mult, 1.5, ALU.add)
                tt(rs[:], rs[:], tmp[:, 2], ALU.mult)

            inverse_rms(1, nt)

            with v.Fori(0, UPC // 2, 1) as b:
                own.enter(b, 10)

                def convolved(j):
                    g_ = j % 2
                    w_ = [lt("cw")[:, bass.ds(b * 12 + (3 * j + k), 1)] for k in range(3)]
                    v.wait_ge(w_used, b * 4 + (U_UP + j + 1))
                    V.tensor_tensor(raw[:, j, 2:2 + T], psum(2 + j % 2), rs[:], ALU.mult).then_inc(raw_ok, 1)
                    v.wait_ge(raw_ok, b * 4 + (j + 3))
                    ts(cv[:, g_], raw[:, j, 2:2 + T], w_[2], ALU.mult, lt("cb")[:, bass.ds(b * 4 + j, 1)], ALU.add)
                    stt(cv[:, g_], raw[:, j, 1:1 + T], w_[1], ALU.mult, cv[:, g_], ALU.add)
                    ins = V.scalar_tensor_tensor(out=cv[:, g_], in0=raw[:, j, 0:T], scalar=w_[0], in1=cv[:, g_],
                                                 op0=ALU.mult, op1=ALU.add)
                    if g_:
                        own.step(ins)
                    else:
                        ins.then_inc(cv_ok, 1)

                for p_ in range(2):
                    blk = bass.ds(b * 2 + p_, 1)
                    convolved(2 * p_)
                    convolved(2 * p_ + 1)
                    v.wait_ge(sl_ok, b * 2 + (p_ + 1))
                    V.tensor_tensor(sl[:], sl[:], cv[:, 1], ALU.mult).then_inc(gg_ok, 1)
                    v.wait_ge(gh_ok, b * 2 + (p_ + 1))
                    V.tensor_tensor(flat2(gtl[:, blk, :]), sl[:], flat2(gth[:, blk, :]).bitcast(F32),
                                    ALU.subtract).then_inc(gl_ok, 1)
            own.leave(UPC // 2)

            v.wait_ge(gl_ok, UPC)
            own.step(V.memset(acc3[:], 0.0))
            with v.Fori(0, 2, 1) as b:
                own.enter(b, 8)
                for j in range(4):
                    xb = flat2(x32[:, bass.ds(b * 4 + j, 1), :])
                    v.wait_ge(w_used, b * 12 + (U_DN + 3 * j + 3))
                    V.tensor_tensor(xb, xb, psum(j % 2), ALU.add).then_inc(x2_ok, 1)
                    v.wait_ge(x2_ok, b * 4 + (j + 3))
                    own.step(V.tensor_tensor(nt3[:, 2], xb, xb, ALU.mult))
                    own.step(V.tensor_tensor(acc3[:], acc3[:], nt3[:, 2], ALU.add))
            own.leave(2)
            V.memset(signal[:, 6:7], 0.0).then_inc(acc_ok, 1)
            inverse_rms(2, nt3)
            for k in range(KT):
                V.scalar_tensor_tensor(out=x32[:, k], in0=x32[:, k], scalar=lt("gfin")[:, k:k + 1], in1=rs[:],
                                       op0=ALU.mult, op1=ALU.mult).then_inc(fin_ok, 1)


        block = ctx.enter_context(nc.Block())

        @block.sync
        def _(sp):
            for i in range(4):
                sp.dma_start(x32[:, 2 * i:2 * i + 2, :], xT[:, 2 * i:2 * i + 2, :]).then_inc(x_in[i], 16)

            def load(u, s, back):
                if back is not None:
                    sp.wait_ge(w_lo, back)
                sp.dma_start(wf[:, s], wst[u]).then_inc(w_in[s], 16)

            for s in range(RING):
                load(s, s, None)
            with sp.Fori(1, NU // RING, 1) as b:
                for s in range(RING):
                    load(b * RING + s, s, b * RING + (s - (RING - 1)))
            for u in range(NU - NU % RING, NU):
                load(u, u % RING, u - (RING - 1))
            store_output(sp)

        @block.gpsimd
        def _(g):
            nc.gpsimd.memset(ones[:], 1.0).then_inc(ones_ok, 1)
            for x_ in (flh, fll):
                nc.gpsimd.memset(x_[:, 16].bitcast(F32), 0.0).then_inc(zero_ok, 1)
            nc.gpsimd.memset(kch[:].bitcast(F32), 0.0).then_inc(zero_ok, 1)
            nc.gpsimd.memset(kcl[:].bitcast(F32), 0.0).then_inc(zero_ok, 1)
            nc.gpsimd.memset(vcs[:].bitcast(F32), 0.0).then_inc(zero_ok, 1)

            def split(s, hi, used):
                g.wait_ge(w_hi, hi)
                if used is not None:
                    g.wait_ge(w_used, used)
                nc.gpsimd.tensor_tensor(wl[:, s], wf[:, s], wh[:, s].bitcast(F32),
                                        ALU.subtract).then_inc(w_lo, 1)

            for s in range(RING):
                split(s, s + 1, None)
            g.wait_ge(hl_ok, KT)
            nc.gpsimd.memset(mtab[:], 0.0).then_inc(zero_ok, 1)
            with g.Fori(1, NU // RING, 1) as b:
                for s in range(RING):
                    split(s, b * RING + (s + 1), b * RING + (s - (RING - 1)))
            for u in range(NU - NU % RING, NU):
                split(u % RING, u + 1, u - (RING - 1))

        @block.scalar
        def _(a):
            own = Count(a, act)
            c_hi, c_out = Count(a, w_hi), Count(a, out_ok)
            a.dma_start(pre[:], pre_d).then_inc(pre_in, 16)
            a.dma_start(cst[:], cst_d).then_inc(cst_in, 16)
            a.dma_start(posi[:], pos_d).then_inc(pos_in, 16)
            a.dma_start(late[:], late_d).then_inc(late_in, 16)

            def prep(u):
                a.wait_ge(w_in[u % RING], 16 * (u // RING + 1))
                if u >= RING:
                    a.wait_ge(w_used, u - RING + 1)
                c_hi.inc(nc.scalar.activation(wh[:, u % RING], wf[:, u % RING], ACT.Copy))

            for k in range(KT):
                if k % 2 == 0:
                    a.wait_ge(x_in[k // 2], 16)
                if k >= 2:
                    a.wait_ge(ss_ok, k - 1)
                nc.scalar.activation(xr[:, k % 2], x32[:, k], ACT.Square).then_inc(sq_ok, 1)
            prep(0)
            a.wait_ge(var_ok, 1)
            nc.scalar.activation(rt[:, 1], rt[:, 0], ACT.Sqrt).then_inc(sd_ok, 1)
            for u in range(1, RING):
                prep(u)
            for k in range(KT):
                a.wait_ge(h_ok, k + 1)
                nc.scalar.activation(hh[:, k], x32[:, k], ACT.Copy).then_inc(hh_ok, 1)
            a.wait_ge(ang_ok, 1)
            for n in range(2):
                nc.scalar.activation(rt[:, n], rt[:, n], ACT.Sin).then_inc(trig_ok, 1)

            def values():
                a.wait_ge(w_used, 3)
                for t in range(NQT):
                    nc.scalar.activation(vst[:, t, :, 0:HD], psum(2 + t)[:, 0:256].rearrange("p (c d) -> p c d", d=HD),
                                         ACT.Copy)
                    nc.scalar.activation(gt[:, t, :], psum(2 + t)[:, 256:VN], ACT.Sigmoid).then_inc(v_hi, 1)

            def stack(n):
                if n:
                    a.wait_ge(fl_ok, 1)
                for kv in range(NKV):
                    src = psum(n % 2)[64 * kv:64 * kv + 64, :]
                    nc.scalar.activation(x2[0:64, kv, :], src, ACT.Copy)
                    ins = nc.scalar.activation(x2[64:128, kv, 0:T - 1], src[:, 1:T], ACT.Copy)
                c_out.inc(ins)

            def feature_done(u):
                a.wait_ge(w_used, u + 1)

            def u_block(i):
                n = place[U_U + i]
                if i >= 2:
                    a.wait_ge(u_put[i - 2], 16)
                c_out.step(nc.scalar.activation(uperm[:, i % 2], psum(n % 2)[:].rearrange("p (c j) -> p j c", j=TC),
                                                ACT.Copy))
                a.dma_start(u_scr[P * i:P * i + P], uperm[:, i % 2]).then_inc(u_put[i], 16)

            def rope_block(u):
                m = rope_place[u]
                if m < 2:
                    a.wait_ge(u_put[2 + m], 16)
                else:
                    a.wait_ge(roped, m - 1)
                c_out.inc(nc.scalar.activation(xr[:, m % 2], psum(place[u] % 2), ACT.Copy))

            def flat_hi(n):
                a.wait_ge(fl_ok, n + 1)
                if n:
                    a.wait_ge(w_used, U_W1K[3] + 1)
                nc.scalar.activation(flh[:, 0:16], fl32[:], ACT.Copy).then_inc(flh_ok, 1)

            def keys(b):
                a.wait_ge(roped, b + 1)
                for kv in range(NKV):
                    for half in range(2):
                        ins = nc.scalar.activation(ksh[64 * half:64 * half + 64, b, kv, :],
                                                   rt[64 * kv:64 * kv + 64, 1, :], ACT.Copy)
                        ins.then_inc(kh_ok, 1)

            def u_load(hf):
                for i in range(2 * hf, 2 * hf + 2):
                    a.wait_ge(u_put[i], 16)
                if hf:
                    a.wait_ge(ym_ok, 1)
                for m in range(TC):
                    a.dma_start(uin[GH * m:GH * m + GH],
                                u_scr.rearrange("(g h) j c -> h j g c", h=GH)[:, TC - 1 - m, 16 * hf:16 * hf + 16, :]
                                ).then_inc(u_get, 16)

            def turned(n):
                a.wait_ge(tr_ok, n + 1)
                if n == 2:
                    a.wait_ge(ym_ok, 1)
                for i in range(2):
                    nc.scalar.activation(ttab[:, n % 2, 4 * i:4 * i + 4, :].rearrange("p a b -> p (a b)"),
                                         psum(3 + i), ACT.Copy).then_inc(t_ok, 1)

            def toeplitz(hf):
                a.wait_ge(kk_ok, hf + 1)
                for q in range(4):
                    nc.scalar.activation(ksb[:, 4 * q:4 * q + 4, :].rearrange("p a b -> p (a b)"),
                                         psum(5)[32 * q:32 * q + GH, :], ACT.Copy).then_inc(kse_ok, 1)
                a.wait_ge(kse_ok, 4 * hf + 4)
                if hf:
                    a.wait_ge(ym_ok, 1)
                else:
                    a.wait_ge(zero_ok, 6)
                for m in range(TC):
                    j = TC - 1 - m
                    a.dma_start(mtab[GH * m:GH * m + GH, :, GH * j:P],
                                ksb[:, :, 0:GH * (TC - j)]).then_inc(m_in, 16)

            def sums(hf):
                a.wait_ge(vm_ok, hf + 1)
                a.wait_ge(l_ok, hf + 1)
                for i in range(2):
                    nc.scalar.activation(vre[:, i].rearrange("p a b -> p (a b)"), psum(3 + i),
                                         ACT.Copy).then_inc(ve_ok, 1)

            def y_store(hf):
                a.wait_ge(ym_ok, hf + 1)
                if hf:
                    a.wait_ge(y_put, 16 * TC)
                else:
                    a.wait_ge(fll_ok, 2)
                for i in range(2):
                    ins = nc.scalar.activation(ysb[:, 8 * i:8 * i + 8, :].rearrange("p a b -> p (a b)"),
                                               psum(3 + i), ACT.Copy)
                    ins.then_inc(ye_ok, 1)
                a.wait_ge(ye_ok, 2 * hf + 2)
                for j in range(TC):
                    a.dma_start(y_scr.rearrange("(g h) j c -> h j g c", h=GH)[:, j, 16 * hf:16 * hf + 16, :],
                                ysb[GH * j:GH * j + GH]).then_inc(y_put, 16)

            def gelu(n):
                a.wait_ge(w_used, (U_W1V if n else U_W1K)[3] + 1)
                nc.scalar.activation(htok[n][:], psum(6)[0:NKV * NCMP, 0:256], ACT.Gelu_apprx_tanh).then_inc(hid_ok, 1)

            def hidden(n):
                a.wait_ge(hidt_ok, n + 1)
                if n:
                    a.wait_ge(cmp_ok, 1)
                for i in range(2):
                    nc.scalar.activation(g32[:, i].rearrange("p a b -> p (a b)"), psum(7)[:, 62 * i:62 * i + 62],
                                         ACT.Copy).then_inc(gelu_ok, 1)

            def kcmp_out():
                a.wait_ge(cmp_ok, 1)
                nc.scalar.activation(kcs[:], psum(5)[:, 0:NCMP], ACT.Copy).then_inc(cmpe_ok, 1)

            def kcmp_hi():
                a.wait_ge(roped, ROPE_CMP + 1)
                a.wait_ge(zero_ok, 5)
                for kv in range(NKV):
                    for half in range(2):
                        nc.scalar.activation(kch[64 * half:64 * half + 64, kv, 0:NCMP],
                                             rt[64 * kv:64 * kv + 64, 1, 0:NCMP], ACT.Copy).then_inc(kh_ok, 1)

            def vcmp_hi():
                a.wait_ge(cmp_ok, 2)
                a.wait_ge(zero_ok, 5)
                for kv in range(NKV):
                    nc.scalar.activation(vcs[NCP * kv:NCP * kv + NCMP, kv, 0:HD],
                                         psum(5)[NCP * kv:NCP * kv + NCMP, 0:HD], ACT.Copy).then_inc(cmpe_ok, 1)

            after = {
                2: [values],
                3: [lambda: stack(0), lambda: flat_hi(0)],
                4: [lambda: stack(1)],
                5: [lambda: u_block(0)], 6: [lambda: u_block(1)], 7: [lambda: u_block(2), lambda: u_load(0)],
                8: [lambda: u_block(3)],
                10: [lambda: rope_block(U_KSL)],
                12: [lambda: rope_block(U_KWN), lambda: turned(0), lambda: keys(0)],
                14: [lambda: rope_block(U_Q[0]), lambda: turned(1), lambda: keys(1)],
                15: [lambda: gelu(0), lambda: flat_hi(1)],
                16: [lambda: rope_block(U_Q[1]), lambda: hidden(0)],
                17: [lambda: sums(0), lambda: toeplitz(0), kcmp_out],
                18: [lambda: rope_block(U_Q[2])],
                20: [kcmp_hi],
                21: [lambda: rope_block(U_Q[3]), lambda: y_store(0), lambda: u_load(1), lambda: turned(2)],
                22: [lambda: gelu(1), lambda: turned(3)],
            }
            for v in range(U_G):
                if v in after:
                    feature_done(v)
                    for f in after[v]:
                        f()
                prep(v + RING)
            hidden(1)
            sums(1)
            vcmp_hi()
            toeplitz(1)
            y_store(1)
            scalar_attention_to_end(a, prep)

        @block.vector
        def _(v):
            own = Count(v, dve)
            V = nc.vector

            def tt(o, x, y, op):
                own.step(V.tensor_tensor(o, x, y, op))

            def ts(o, x, s1, op1, s2=None, op2=None):
                if op2 is None:
                    own.step(V.tensor_scalar(o, x, s1, None, op1))
                else:
                    own.step(V.tensor_scalar(o, x, s1, s2, op1, op2))

            def stt(o, x, s1, op1, y, op2):
                own.step(V.scalar_tensor_tensor(out=o, in0=x, scalar=s1, in1=y, op0=op1, op1=op2))

            names = ["dt", "ar", "th", "k", "r", "e", "t0", "t1", "s", "co", "c1", "sn", "cs", "gr", "gi", "fr", "fi",
                     "den", "rho"] + [f"u{2 ** i}{x}" for i in range(6) for x in "ri"]
            S = {n: sm[:, i, :] for i, n in enumerate(names)}
            assert len(names) <= 32

            def horner(o, x, coefs):
                ts(o, x, coefs[0], ALU.mult)
                for c_ in coefs[1:]:
                    stt(o, o, c_, ALU.add, x, ALU.mult)

            v.wait_ge(pre_in, 16)
            f = [1.0 / math.factorial(i) for i in range(12)]
            exp_c = [f[8], f[7], f[6], f[5], f[4], f[3], f[2], f[1]]
            ts(S["t0"], pr("ldt"), -150.0, ALU.max, 130.0, ALU.min)
            ts(S["k"], S["t0"], 1.0 / math.log(2), ALU.mult, MAGIC, ALU.add)
            ts(S["k"], S["k"], MAGIC, ALU.subtract)
            stt(S["r"], S["k"], -LN2H, ALU.mult, S["t0"], ALU.add)
            stt(S["r"], S["k"], -LN2L, ALU.mult, S["r"], ALU.add)
            horner(S["e"], S["r"], exp_c)
            ts(S["t0"], S["k"], 0.5, ALU.mult, MAGIC, ALU.add)
            ts(S["t0"], S["t0"], MAGIC, ALU.subtract)
            tt(S["t1"], S["k"], S["t0"], ALU.subtract)
            for n in ("t0", "t1"):
                ts(S[n].bitcast(I32), S[n], 127.0, ALU.add, float(2 ** 23), ALU.mult)
            stt(S["dt"], S["e"], 1.0, ALU.add, S["t0"], ALU.mult)
            tt(S["dt"], S["dt"], S["t1"], ALU.mult)
            tt(S["ar"], pr("are"), S["dt"], ALU.mult)
            ts(S["ar"], S["ar"], -104.0, ALU.max, 89.0, ALU.min)
            ts(S["r"], S["ar"], 1.0 / 256, ALU.mult)
            horner(S["e"], S["r"], exp_c)
            for _ in range(8):
                stt(S["e"], S["e"], 2.0, ALU.add, S["e"], ALU.mult)
            v.wait_ge(ss_ok, KT)
            c_var = Count(v, var_ok)
            c_var.step(V.tensor_scalar(rt[:, 0], psum(7), 1.0 / D, EPS, ALU.mult, ALU.add))
            v.wait_ge(sd_ok, 1)
            own.step(V.reciprocal(cosT[:], rt[:, 1]))
            tt(sinT[:], cosT[:], cosT[:], ALU.mult)
            tt(sinT[:], sinT[:], rt[:, 0], ALU.mult)
            ts(sinT[:], sinT[:], -0.5, ALU.mult, 1.5, ALU.add)
            tt(cosT[:], cosT[:], sinT[:], ALU.mult)
            v.wait_ge(late_in, 16)
            c_h, c_hl = Count(v, h_ok), Count(v, hl_ok)

            def h_lo(k):
                v.wait_ge(hh_ok, k + 1)
                c_hl.inc(V.tensor_tensor(hl[:, k], x32[:, k], hh[:, k].bitcast(F32), ALU.subtract))

            for k in range(KT):
                c_h.inc(V.scalar_tensor_tensor(out=x32[:, k], in0=x32[:, k], scalar=lt("gmix")[:, k:k + 1],
                                               in1=cosT[:], op0=ALU.mult, op1=ALU.mult))
                if k:
                    h_lo(k - 1)
            h_lo(KT - 1)
            c_hl.wait()

            v.wait_ge(pos_in, 16)
            v.wait_ge(cst_in, 16)
            own.step(V.tensor_copy(sinT[:], posi[:]))
            ts(sinT[:], sinT[:], c("freq"), ALU.mult)
            ts(cosT[:], sinT[:], 1 / TWO_PI, ALU.mult, MAGIC, ALU.add)
            ts(cosT[:], cosT[:], MAGIC, ALU.subtract)
            for part in (C1, C2, C3):
                stt(sinT[:], cosT[:], -part, ALU.mult, sinT[:], ALU.add)
            ts(rt[:, 0], sinT[:], 0.5, ALU.mult)
            ts(rt[:, 1], rt[:, 0], -1.0, ALU.mult)
            tt(rt[:, 1], rt[:, 1], rt[:, 0], ALU.max)
            V.tensor_scalar(rt[:, 1], rt[:, 1], -1.0, math.pi / 2, ALU.mult, ALU.add).then_inc(ang_ok, 1)
            v.wait_ge(trig_ok, 2)
            stt(sinT[:], rt[:, 0], 2.0, ALU.mult, rt[:, 1], ALU.mult)
            stt(cosT[:], rt[:, 0], -2.0, ALU.mult, rt[:, 0], ALU.mult)
            ts(cosT[:], cosT[:], 1.0, ALU.add)
            own.step(V.tensor_copy(identb[:], c("ident")))
            V.tensor_copy(maskb[:], c("causal")).then_inc(bf_ok, 1)

            for t in range(NQT):
                v.wait_ge(v_hi, t + 1)
                V.tensor_tensor(vst[:, t, :, HD:P], psum(2 + t)[:, 0:256].rearrange("p (c d) -> p c d", d=HD),
                                vst[:, t, :, 0:HD].bitcast(F32), ALU.subtract).then_inc(v_lo, 1)

            def flat(n):
                v.wait_ge(out_ok, n + 1)
                if n:
                    v.wait_ge(fll_ok, 1)
                pe = pr("pev" if n else "pek").unsqueeze(2).to_broadcast([P, 16, NCMP])
                for kv in range(NKV):
                    span = x2[:, kv, :]
                    src = bass.AP(tensor=span.tensor, offset=span.offset, ap=[list(span.ap[0]), [2, 16], [16, NCMP]])
                    (c_fl if kv else own).step(V.tensor_tensor(fl32[:, :, kv, :], src, pe, ALU.add))

            def flat_lo(n):
                v.wait_ge(flh_ok, n + 1)
                V.tensor_tensor(fll[:, 0:16], fl32[:], flh[:, 0:16].bitcast(F32), ALU.subtract).then_inc(fll_ok, 1)

            c_fl, c_w2, c_l, c_xs, c_roped = (Count(v, s_) for s_ in (fl_ok, w2_ok, l_ok, xs_ok, roped))
            flat(0)
            flat_lo(0)
            flat(1)

            tt(S["th"], pr("aim"), S["dt"], ALU.mult)
            ts(S["k"], S["th"], 1 / TWO_PI, ALU.mult, MAGIC, ALU.add)
            ts(S["k"], S["k"], MAGIC, ALU.subtract)
            for part in (C1, C2, C3):
                stt(S["th"], S["k"], -part, ALU.mult, S["th"], ALU.add)
            ts(S["th"], S["th"], 0.5, ALU.mult)
            tt(S["r"], S["th"], S["th"], ALU.mult)
            horner(S["s"], S["r"], [1 / math.factorial(13), -1 / math.factorial(11), f[9], -f[7], f[5], -f[3]])
            stt(S["s"], S["s"], 1.0, ALU.add, S["th"], ALU.mult)
            horner(S["co"], S["r"], [1 / math.factorial(12), -f[10], f[8], -f[6], f[4], -f[2]])
            ts(S["co"], S["co"], 1.0, ALU.add)
            stt(S["c1"], S["s"], -2.0, ALU.mult, S["s"], ALU.mult)
            stt(S["sn"], S["s"], 2.0, ALU.mult, S["co"], ALU.mult)
            ts(S["cs"], S["c1"], 1.0, ALU.add)
            tt(S["gr"], S["e"], S["cs"], ALU.mult)
            tt(S["gr"], S["gr"], S["c1"], ALU.add)
            stt(S["gi"], S["e"], 1.0, ALU.add, S["sn"], ALU.mult)
            tt(S["t0"], pr("are"), pr("are"), ALU.mult)
            tt(S["t1"], pr("aim"), pr("aim"), ALU.mult)
            tt(S["t0"], S["t0"], S["t1"], ALU.add)
            own.step(V.reciprocal(S["den"], S["t0"]))
            tt(S["fr"], S["gr"], pr("are"), ALU.mult)
            tt(S["t0"], S["gi"], pr("aim"), ALU.mult)
            tt(S["fr"], S["fr"], S["t0"], ALU.add)
            tt(S["fr"], S["fr"], S["den"], ALU.mult)
            tt(S["fi"], S["gi"], pr("are"), ALU.mult)
            tt(S["t0"], S["gr"], pr("aim"), ALU.mult)
            tt(S["fi"], S["fi"], S["t0"], ALU.subtract)
            tt(S["fi"], S["fi"], S["den"], ALU.mult)
            ts(S["rho"], S["e"], 1.0, ALU.add)
            for _ in range(3):
                tt(S["rho"], S["rho"], S["rho"], ALU.mult)
            def square(zr, zi, xr_, xi):
                tt(S["t0"], xr_, xr_, ALU.mult)
                tt(S["t1"], xi, xi, ALU.mult)
                stt(zi, xr_, 2.0, ALU.mult, xi, ALU.mult)
                tt(zr, S["t0"], S["t1"], ALU.subtract)

            square(S["r"], S["k"], S["cs"], S["sn"])
            square(S["co"], S["s"], S["r"], S["k"])
            square(S["u1r"], S["u1i"], S["co"], S["s"])
            for i in range(5):
                square(S[f"u{2 ** (i + 1)}r"], S[f"u{2 ** (i + 1)}i"], S[f"u{2 ** i}r"], S[f"u{2 ** i}i"])
            own.step(V.memset(pw[:, 0, 0, :], 1.0))
            own.step(V.memset(pw[:, 1, 0, :], 0.0))
            ts(pw[:, 0, 1, :], S["gr"], 1.0, ALU.add)
            ts(pw[:, 1, 1, :], S["gi"], 0.0, ALU.add)
            prod = atmp[:, 0:4 * NP].rearrange("p (a b) -> p a b", b=NP)

            def power(lo, hi, by):
                n = hi - lo + 1
                xr_, xi = pw[:, 0, lo:hi + 1, :], pw[:, 1, lo:hi + 1, :]
                br, bi = (pw[:, i, by, :].unsqueeze(1).to_broadcast([P, n, NP]) for i in range(2))
                zr, zi = pw[:, 0, lo + by:hi + by + 1, :], pw[:, 1, lo + by:hi + by + 1, :]
                tt(prod[:, 0:n], xi, bi, ALU.mult)
                tt(zr, xr_, br, ALU.mult)
                tt(zr, zr, prod[:, 0:n], ALU.subtract)
                tt(prod[:, 0:n], xi, br, ALU.mult)
                tt(zi, xr_, bi, ALU.mult)
                tt(zi, zi, prod[:, 0:n], ALU.add)

            power(1, 1, 1)
            power(1, 2, 2)
            power(1, 4, 4)
            b3 = [pr(n).rearrange("p (a b) -> p a b", b=GH) for n in ("bre", "bim")]
            fr, fi = (S[n].unsqueeze(2).to_broadcast([P, NP, GH]) for n in ("fr", "fi"))
            t2 = atmp[:, 0:NP * GH].rearrange("p (a b) -> p a b", b=GH)
            tt(bbar[:, 0], b3[0], fr, ALU.mult)
            tt(t2, b3[1], fi, ALU.mult)
            tt(bbar[:, 0], bbar[:, 0], t2, ALU.subtract)
            tt(bbar[:, 1], b3[1], fr, ALU.mult)
            tt(t2, b3[0], fi, ALU.mult)
            tt(bbar[:, 1], bbar[:, 1], t2, ALU.add)
            own.step(V.memset(bb[:], 0.0))
            for e in range(2):
                rows = slice(64 * e, 64 * e + 64)
                own.step(V.tensor_copy(bb[rows, :, e], bbar[rows]))

            def cplx(dst_r, dst_i, pr_, pi_, qr, qi, tmp, negate=False, last=own):
                tt(dst_r, pr_, qr, ALU.mult)
                tt(tmp, pi_, qi, ALU.mult)
                tt(dst_r, dst_r, tmp, ALU.subtract)
                tt(dst_i, pr_, qi, ALU.mult)
                tt(tmp, pi_, qr, ALU.mult)
                if negate:
                    last.step(V.scalar_tensor_tensor(out=dst_i, in0=dst_i, scalar=-1.0, in1=tmp, op0=ALU.mult,
                                                     op1=ALU.subtract))
                else:
                    last.step(V.tensor_tensor(dst_i, dst_i, tmp, ALU.add))

            def input_table(hf):
                pairs = slice(HP * hf, HP * hf + HP)
                if hf:
                    v.wait_ge(m_in, 16 * TC)
                tmp = atmp[:, 0:HP * TC * GH].rearrange("p (a b c) -> p a b c", a=HP, b=TC)
                w = [w2t[:, i].rearrange("p a (b c) -> p a b c", b=TC) for i in range(2)]
                pq = [pw[:, i, 0:TC, pairs].rearrange("p k a -> p a k").unsqueeze(3).to_broadcast([P, HP, TC, GH])
                      for i in range(2)]
                q = [bbar[:, i, pairs, :].unsqueeze(2).to_broadcast([P, HP, TC, GH]) for i in range(2)]
                cplx(w[0], w[1], pq[0], pq[1], q[0], q[1], tmp, last=c_w2)

            def output_table(hf):
                pairs = slice(HP * hf, HP * hf + HP)
                if hf:
                    v.wait_ge(ym_ok, 1)
                tmp = atmp[:, 0:HP * (TC + 1) * GH].rearrange("p (a b c) -> p a b c", a=HP, b=TC + 1)
                pq = [pw[:, i, :, pairs].rearrange("p k a -> p a k").unsqueeze(3).to_broadcast([P, HP, TC + 1, GH])
                      for i in range(2)]
                q = [pr(n).rearrange("p (a b) -> p a b", b=GH)[:, pairs, :].unsqueeze(2).to_broadcast(
                    [P, HP, TC + 1, GH]) for n in ("cre", "cim")]
                cplx(ltab[:, 0], ltab[:, 1], pq[0], pq[1], q[0], q[1], tmp, negate=True, last=c_l)

            def phases(hf):
                pairs = slice(HP * hf, HP * hf + HP)
                own.step(V.memset(rtab[:, 0, :, 0:1], 1.0))
                own.step(V.memset(rtab[:, 1, :, 0:1], 0.0))
                for i in range(6):
                    m = 2 ** i
                    u_ = [S[f"u{m}{x}"][:, pairs].unsqueeze(2).to_broadcast([P, HP, m]) for x in "ri"]
                    lo, hi = slice(0, m), slice(m, 2 * m)
                    cplx(rtab[:, 0, :, hi], rtab[:, 1, :, hi], rtab[:, 0, :, lo], rtab[:, 1, :, lo], u_[0], u_[1],
                         rt[:, 0].rearrange("p (a b) -> p a b", a=HP)[:, :, lo])

            def skips():
                own.step(V.memset(skip[:], 0.0))
                V.tensor_tensor(skip[0:GH], c("eye16", slice(0, GH)).unsqueeze(1).to_broadcast([GH, G, GH]),
                                pr("d", slice(0, GH)).unsqueeze(2).to_broadcast([GH, G, GH]),
                                ALU.mult).then_inc(sk_ok, 1)

            def states(hf):
                v.wait_ge(ve_ok, 2 * hf + 2)
                R, I = rtab[:, 0], rtab[:, 1]
                z = [xs[:, 0, 0], xs[:, 1, 0]]
                t3 = rt[:, 0].rearrange("p (a b) -> p a b", a=HP)
                tt(z[0], R, vre[:, 0], ALU.mult)
                tt(t3, I, vre[:, 1], ALU.mult)
                tt(z[0], z[0], t3, ALU.add)
                tt(z[1], R, vre[:, 1], ALU.mult)
                tt(t3, I, vre[:, 0], ALU.mult)
                tt(z[1], z[1], t3, ALU.subtract)
                ts(t3, S["rho"][:, HP * hf:HP * hf + HP].unsqueeze(2).to_broadcast([P, HP, NC]), 1.0, ALU.mult)
                own.step(V.memset(t3[:, :, 0:1], 0.0))
                for i in range(2):
                    own.step(V.tensor_tensor_scan(vre[:, i].rearrange("p a b -> p (a b)"), rt[:, 0],
                                                  z[i].rearrange("p a b -> p (a b)"), 0.0, ALU.mult, ALU.add))
                own.inc(V.memset(xs[0:64, :, 1], 0.0))
                cplx(xs[:, 0, 0, :, 1:NC], xs[:, 1, 0, :, 1:NC], vre[:, 0, :, 0:NC - 1], vre[:, 1, :, 0:NC - 1],
                     R[:, :, 0:NC - 1], I[:, :, 0:NC - 1], t3[:, :, 0:NC - 1])
                own.step(V.memset(xs[:, :, 0, :, 0:1], 0.0))
                for i in range(2):
                    own.inc(V.tensor_copy(xs[64:P, i, 1], xs[64:P, i, 0]))
                own.wait()
                c_xs.step(V.memset(xs[64:P, :, 0], 0.0))

            def rope(n, dst):
                v.wait_ge(perm_ok, n + 1)
                w = NCMP if n == ROPE_CMP else T
                src = kcs[:] if n == ROPE_CMP else xr[:, (n - (n > ROPE_CMP)) % 2]
                at_ = slice(31, None, 16) if n == ROPE_CMP else slice(None)
                tt(rt[:, 0, 0:w], src, cosT[:, at_], ALU.mult)
                tt(dst, psum(2)[:, 0:w], sinT[:, at_], ALU.mult)
                c_roped.step(V.tensor_tensor(dst, dst, rt[:, 0, 0:w], ALU.add))

            def keys_lo(b):
                v.wait_ge(kh_ok, 4 * b + 4)
                for kv in range(NKV):
                    rows, other = slice(64 * kv, 64 * kv + 64), slice(64 - 64 * kv, 128 - 64 * kv)
                    own.step(V.tensor_tensor(ksl[rows, b, kv, :], rt[rows, 1, :], ksh[rows, b, kv, :].bitcast(F32),
                                             ALU.subtract))
                    own.inc(V.tensor_copy(ksl[other, b, kv, :], ksl[rows, b, kv, :].bitcast(F32)))
                own.wait()

            def compressed_keys_lo():
                v.wait_ge(kh_ok, 12)
                for kv in range(NKV):
                    rows, other = slice(64 * kv, 64 * kv + 64), slice(64 - 64 * kv, 128 - 64 * kv)
                    own.step(V.tensor_tensor(kcl[rows, kv, 0:NCMP], rt[rows, 1, 0:NCMP],
                                             kch[rows, kv, 0:NCMP].bitcast(F32), ALU.subtract))
                    own.step(V.tensor_copy(kcl[other, kv, 0:NCMP], kcl[rows, kv, 0:NCMP].bitcast(F32)))

            def compressed_values_lo():
                v.wait_ge(cmpe_ok, 3)
                for kv in range(NKV):
                    rows = slice(NCP * kv, NCP * kv + NCMP)
                    V.tensor_tensor(vcs[rows, kv, HD:P], psum(5)[rows, 0:HD], vcs[rows, kv, 0:HD].bitcast(F32),
                                    ALU.subtract).then_inc(vc_ok, 1)

            input_table(0)
            rope(0, rt[:, 1])
            keys_lo(0)
            skips()
            output_table(0)
            rope(1, rt[:, 1])
            keys_lo(1)
            flat_lo(1)
            phases(0)
            rope(2, q32[:, 0])
            rope(3, q32[:, 1])
            states(0)
            rope(4, rt[:, 1, 0:NCMP])
            input_table(1)
            compressed_keys_lo()
            rope(5, q32[:, 2])
            phases(1)
            output_table(1)
            rope(6, q32[:, 3])
            compressed_values_lo()
            states(1)
            vector_attention_to_end(v, own, tt, ts, stt)

        @block.tensor
        def _(pe):
            M = nc.tensor

            def ready(u):
                pe.wait_ge(w_lo, u + 1)

            def three(out, s_hi, s_lo, m_hi, m_lo, first, last):
                M.matmul(out, s_hi, m_hi, start=first, stop=False)
                M.matmul(out, s_hi, m_lo, start=False, stop=False)
                return M.matmul(out, s_lo, m_hi, start=False, stop=last)

            pe.wait_ge(ones_ok, 1)
            for k in range(KT):
                pe.wait_ge(sq_ok, k + 1)
                M.matmul(psum(7), ones[:], xr[:, k % 2], start=(k == 0), stop=(k == KT - 1)).then_inc(ss_ok, 1)

            for m in range(3):
                ready(U_V + m)
                for kk in range(3 if m < 2 else 2):
                    k = 3 * m + kk
                    pe.wait_ge(hl_ok, k + 1)
                    w_ = [b_[:, (U_V + m) % RING].rearrange("p a b -> p (a b)")[:, kk * VN:(kk + 1) * VN]
                          for b_ in (wh, wl)]
                    for t in range(NQT):
                        tok = slice(P * t, P * t + P)
                        ins = three(psum(2 + t)[:, 0:VN], hh[:, k, tok], hl[:, k, tok], w_[0], w_[1],
                                    k == 0, k == KT - 1)
                ins.then_inc(w_used, 1)

            def feature(u):
                n = place[u]
                ready(u)
                if n >= 2:
                    pe.wait_ge(out_ok, n - 1)
                for k in range(KT):
                    ins = three(psum(n % 2), wh[:, u % RING, k], wl[:, u % RING, k], hh[:, k], hl[:, k],
                                k == 0, k == KT - 1)
                ins.then_inc(w_used, 1)

            def compress(u, n, m):
                ready(u)
                if m == 0:
                    pe.wait_ge(fll_ok, n + 1)
                    if n:
                        pe.wait_ge(hid_ok, 1)
                    else:
                        pe.wait_ge(zero_ok, 2)
                for i in range(4):
                    w_ = [b_[:, u % RING].rearrange("p a b -> p (a b)")[:, 256 * i:256 * i + 256] for b_ in (wh, wl)]
                    x_ = [b_[:, 4 * m + i:4 * m + i + 2].rearrange("p c a b -> p (c a b)") for b_ in (flh, fll)]
                    ins = three(psum(6)[0:4 * NCMP, 0:256], x_[0], x_[1], w_[0], w_[1], m == 0 and i == 0,
                                m == 3 and i == 3)
                ins.then_inc(w_used, 1)

            def compress_turn(n):
                pe.wait_ge(hid_ok, n + 1)
                rows = slice(0, NKV * NCMP)
                for i in range(2):
                    ins = M.matmul(psum(7)[:, 62 * i:62 * i + 62], htok[n][:, P * i:P * i + P],
                                   cst[rows, CST["ident"][0]:CST["ident"][0] + NKV * NCMP], start=True, stop=True)
                ins.then_inc(hidt_ok, 1)

            def compress_out(n):
                pe.wait_ge(gelu_ok, 2 * n + 2)
                if n:
                    pe.wait_ge(cmpe_ok, 1)
                else:
                    pe.wait_ge(kse_ok, 4)
                w2 = pr("w2v" if n else "w2k").rearrange("p (a b) -> p a b", b=HD)
                for kv in range(NKV):
                    for hc in range(2):
                        if n:
                            ins = M.matmul(psum(5)[NCP * kv:NCP * kv + NCMP, 0:HD], g32[:, hc, kv, :], w2[:, hc, :],
                                           start=(hc == 0), stop=(hc == 1))
                        else:
                            ins = M.matmul(psum(5)[64 * kv:64 * kv + 64, 0:NCMP], w2[:, hc, :], g32[:, hc, kv, :],
                                           start=(hc == 0), stop=(hc == 1))
                ins.then_inc(cmp_ok, 1)

            def partner(n):
                src = kcs[:] if n == ROPE_CMP else xr[:, (n - (n > ROPE_CMP)) % 2]
                w = NCMP if n == ROPE_CMP else T
                if n == ROPE_CMP:
                    pe.wait_ge(cmpe_ok, 1)
                else:
                    pe.wait_ge(out_ok, 6 + n - (n > ROPE_CMP) + 1)
                if n:
                    pe.wait_ge(roped, n)
                else:
                    pe.wait_ge(v_lo, NQT)
                    pe.wait_ge(cst_in, 16)
                M.matmul(psum(2)[:, 0:w], c("perm"), src, start=True, stop=True).then_inc(perm_ok, 1)

            def turn(n):
                if n == 0:
                    pe.wait_ge(v_lo, NQT)
                    pe.wait_ge(cst_in, 16)
                pe.wait_ge(w2_ok, n // 2 + 1)
                if n % 2:
                    pe.wait_ge(t_ok, 2 * n)
                elif n:
                    pe.wait_ge(ye_ok, 2)
                for i in range(HP):
                    ins = M.transpose(psum(3 + i // 4)[:, P * (i % 4):P * (i % 4) + P], w2t[:, n % 2, i], c("ident"))
                ins.then_inc(tr_ok, 1)

            def lag_blocks(hf):
                pe.wait_ge(l_ok, hf + 1)
                pe.wait_ge(sk_ok, 1)
                if hf:
                    pe.wait_ge(vc_ok, 2)
                for gl in range(2 * HP):
                    q, col = gl // 4, P * (gl % 4)
                    for i in range(2):
                        ins = M.matmul(psum(5)[32 * q:32 * q + GH, col:col + P],
                                       bb[:, i, gl % 2, HP * hf + gl // 2, :],
                                       ltab[:, i, gl // 2, 0:TC, :].rearrange("p a b -> p (a b)"),
                                       start=(i == 0), stop=False)
                    ins = M.matmul(psum(5)[32 * q:32 * q + GH, col:col + GH], c("eye16"),
                                   skip[:, 2 * HP * hf + gl, :], start=False, stop=True)
                ins.then_inc(kk_ok, 1)

            def chunk_sums(hf):
                pe.wait_ge(t_ok, 4 * hf + 4)
                pe.wait_ge(u_get, 16 * TC * (hf + 1))
                for i in range(2):
                    for gl in range(2 * HP):
                        e, hp = gl % 2, gl // 2
                        ins = M.matmul(psum(3 + i)[64 * e:64 * e + 64, NC * hp:NC * hp + NC],
                                       ttab[:, i, hp, 64 * e:64 * e + 64], uin[:, gl, :], start=True, stop=True)
                ins.then_inc(vm_ok, 1)

            def ssm_out(hf):
                pe.wait_ge(m_in, 16 * TC * (hf + 1))
                pe.wait_ge(xs_ok, hf + 1)
                pe.wait_ge(ve_ok, 2 * hf + 2)
                for hp in range(HP):
                    at_ = NC * (2 * hp % 8)
                    out = psum(3 + hp // 4)[:, at_:at_ + 2 * NC]
                    for i in range(2):
                        M.matmul(out, ltab[:, i, hp, 1:TC + 1, :].rearrange("p a b -> p (a b)"),
                                 xs[:, i, :, hp, :], start=(i == 0), stop=False)
                    for e in range(2):
                        ins = M.matmul(out[:, NC * e:NC * e + NC], mtab[:, 2 * hp + e, :], uin[:, 2 * hp + e, :],
                                       start=False, stop=(e == 1))
                ins.then_inc(ym_ok, 1)

            for u in [U_KC, U_VC] + [U_U + i for i in range(4)]:
                feature(u)
            compress(U_W1K[0], 0, 0)
            feature(U_KSL)
            compress(U_W1K[1], 0, 1)
            partner(0)
            feature(U_KWN)
            turn(0)
            compress(U_W1K[2], 0, 2)
            partner(1)
            feature(U_Q[0])
            turn(1)
            compress(U_W1K[3], 0, 3)
            lag_blocks(0)
            feature(U_Q[1])
            compress_turn(0)
            partner(2)
            chunk_sums(0)
            compress(U_W1V[0], 1, 0)
            compress_out(0)
            partner(3)
            feature(U_Q[2])
            compress(U_W1V[1], 1, 1)
            compress(U_W1V[2], 1, 2)
            partner(4)
            feature(U_Q[3])
            ssm_out(0)
            partner(5)
            turn(2)
            compress(U_W1V[3], 1, 3)
            turn(3)
            partner(6)
            compress_turn(1)
            chunk_sums(1)
            compress_out(1)
            lag_blocks(1)
            ssm_out(1)
            tensor_attention_to_end(pe, ready, three)


def _blocks(w):
    return w.reshape(-1, P, w.shape[1]).transpose(1, 0, 2)


def _pack(i):
    g = {n: np.asarray(a) for n, a in i.items()}
    w_in = g["w_in"][0]
    off = np.cumsum([0, 512] + 6 * [128] + [24, 512, 1024, 1024])
    q0, kc0, vc0, ks0, vs0, kw0, vw0, ng0, u0, ga0, gb0 = off[:11]
    wst = np.zeros((NU, P, KT * P), np.float32)

    def put(u, a, at=0):
        a = np.asarray(a).reshape(P, -1)
        wst[u][:, at:at + a.shape[1]] = a

    wb = _blocks(w_in)
    gates = [ng0 + (kv * REP + r) * 3 + br for br in range(3) for r in range(REP) for kv in range(NKV)]
    vcols = np.r_[vs0:vs0 + 128, vw0:vw0 + 128, gates]
    for m in range(3):
        put(U_V + m, wb[:, 3 * m:min(3 * m + 3, KT)][:, :, vcols])
    for u, c0 in [(U_KC, kc0), (U_VC, vc0), (U_KSL, ks0), (U_KWN, kw0)] + [(U_U + n, u0 + P * n) for n in range(4)]:
        put(u, wb[:, :, c0:c0 + P])
    for r, u in enumerate(U_Q):
        cols = np.r_[[q0 + (kv * REP + r) * HD + d for kv in range(NKV) for d in range(HD)]]
        put(u, wb[:, :, cols])
    for j in range(KT):
        put(U_G + j, wb[:, :, ga0 + P * j:ga0 + P * j + P])
        put(U_G + KT + j, wb[:, :, gb0 + P * j:gb0 + P * j + P])
    for us, name in ((U_W1K, "cmp_k_w1"), (U_W1V, "cmp_v_w1")):
        w1 = _blocks(g[name][0])
        for m, u in enumerate(us):
            put(u, w1[:, 4 * m:4 * m + 4])
    glu = _blocks(g["ssm_w_glu"][0])
    for n in range(4):
        put(U_GLU + n // 2, glu[:, :, P * n:P * n + P], 4 * P * (n % 2))
    rows = [(kv * REP + r) * HD + d for r in range(REP) for kv in range(NKV) for d in range(HD)]
    pa, pb = _blocks(g["w_proj_a"][0][rows]), _blocks(g["w_proj_b"][0])
    wo, up, dn = _blocks(g["w_out"][0]), _blocks(g["w_up"][0]), _blocks(g["w_down"][0])
    for o in range(KT):
        cols = slice(P * o, P * o + P)
        put(U_M + o, pa[:, :, cols])
        put(U_M + o, pb[:, :, cols], 4 * P)
        put(U_O + o, wo[:, :, cols])
        for m in range(3):
            put(U_DN + 3 * o + m, dn[:, 8 * m:min(8 * m + 8, UPC), cols])
    for j in range(UPC):
        put(U_UP + 2 * j, up[:, :, P * j:P * j + P])
        put(U_UP + 2 * j + 1, up[:, :, DFF + P * j:DFF + P * j + P])

    cst = np.zeros((P, N_CST), np.float32)

    def cput(name, a):
        a = np.asarray(a, np.float32).reshape(np.shape(a)[0], -1)
        cst[:a.shape[0], CST[name][0]:CST[name][1]] = a

    cput("ident", np.eye(P))
    perm = np.zeros((P, P))
    for kv in range(NKV):
        for d in range(8):
            perm[64 * kv + d + 8, 64 * kv + d] = -1.0
            perm[64 * kv + d, 64 * kv + d + 8] = 1.0
    cput("perm", perm)
    n = np.arange(P)
    cput("causal", np.where(n[None, :] <= n[:, None], 0.0, NEG))
    t = np.arange(NQT)[None, :, None] * P + n[:, None, None]
    ok = (np.arange(NCP)[None, None, :] * 16 + 31 <= t) & (np.arange(NCP) < NCMP)
    ok = np.broadcast_to(ok[:, :, None, :], (P, NQT, NKV, NCP))
    cput("cadd", np.where(ok, 0.0, NEG))
    cput("c01", ok.astype(np.float32))
    freq = 500000.0 ** (-np.arange(0, 16, 2) / 16)
    row = np.concatenate([freq, freq, np.zeros(HD - 16)])
    cput("freq", np.tile(row, 2)[:, None])
    cput("eye16", np.eye(GH))

    pre = np.zeros((P, N_PRE), np.float32)

    def pput(name, a):
        a = np.asarray(a).reshape(np.shape(a)[0], -1)
        pre[:a.shape[0], PRE[name][0]:PRE[name][1]] = a

    def pairs(a):
        return a.reshape(NP, 2 * NST, *a.shape[2:]).swapaxes(0, 1)

    pput("ldt", pairs(np.broadcast_to(g["ssm_log_dt"][0][:, None], (G, NST))))
    pput("are", pairs(g["ssm_a_re"][0]))
    pput("aim", pairs(g["ssm_a_im"][0]))
    pput("bre", pairs(g["ssm_b_re"][0]))
    pput("bim", pairs(g["ssm_b_im"][0]))
    pput("cre", pairs(g["ssm_c_re"][0].swapaxes(1, 2)))
    pput("cim", pairs(g["ssm_c_im"][0].swapaxes(1, 2)))
    pput("w2k", _blocks(g["cmp_k_w2"][0]))
    pput("w2v", _blocks(g["cmp_v_w2"][0]))
    pput("pek", g["cmp_k_pe"][0].reshape(16, P).T)
    pput("pev", g["cmp_v_pe"][0].reshape(16, P).T)
    pput("d", g["ssm_d"][0].reshape(G, GH).T)

    late = np.zeros((P, N_LATE), np.float32)

    def lput(name, a):
        late[:, LATE[name][0]:LATE[name][1]] = np.asarray(a).reshape(P, -1)

    lput("gmix", g["norm_mix"][0].reshape(KT, P).T)
    lput("gffn", g["norm_ffn"][0].reshape(KT, P).T)
    lput("gfin", g["norm_final"].reshape(KT, P).T)
    order = [P * j + o for j in range(UPC) for o in (0, DFF)]
    lput("cw", np.stack([g["conv_w"][0][:, o:o + P].T for o in order], 1))
    lput("cb", np.stack([g["conv_b"][0][o:o + P] for o in order], 1))
    xT = np.ascontiguousarray(g["x"][0].T.reshape(KT, P, T).transpose(1, 0, 2))
    pos = np.ascontiguousarray(np.broadcast_to(g["positions"][0].astype(np.int32), (P, T)))
    return {"wst": wst.reshape(NU, P, KT, P), "xT": xT, "cst": cst, "pre": pre, "late": late, "pos": pos}


_DT = {"pos": I32}
_ORDER = ("wst", "xT", "cst", "pre", "late", "pos")


def _program(nc, arrays):
    args = [nc.dram_tensor(f"in_{n}", arrays[n].shape, _DT.get(n, F32), kind="ExternalInput").ap() for n in _ORDER]
    out = nc.dram_tensor("out", (P, KT, T), F32, kind="ExternalOutput").ap()
    build(nc, *args, out)


def kernel(**inputs):
    import concourse.bacc as _bacc
    from concourse.bass_utils import run_bass_kernel_spmd as _run

    arrays = _pack(inputs)
    nc = _bacc.Bacc("TRN2", target_bir_lowering=False, num_devices=1)
    _program(nc, arrays)
    r = _run(nc, [{f"in_{n}": a for n, a in arrays.items()}], core_ids=[0])
    outT = np.asarray(r.results[0]["out"])
    return np.ascontiguousarray(outT.transpose(2, 1, 0).reshape(1, T, D))
```
